# Optimizing a Trainium2 kernel written in Bass

```python
import jax, jax.numpy as jnp
from jax import lax
import numpy as np

D_MODEL = 1024
BATCH = 1
SEQ = 512
DEPTH = 2
DEC_BATCH = 1
DEC_SEQ = 32
PAST_LEN = 256

CHUNK = 64
A_PAST_CHUNKS = 8
N_HEADS_A = 8
HEAD_DIM_A = 64
REL_MIN = -(CHUNK - 1)
REL_MAX = 2 * CHUNK
N_REL = REL_MAX - REL_MIN + 1
N_HEADS_B = 4
HEAD_K_B = 64
HEAD_V_B = 128
GATE_RANK = 16
GATE_NORM = 16.0
CONV_W = 31
D_FF = 4 * D_MODEL
N_AB_LAYERS = (DEPTH + 1) // 2
N_C_LAYERS = DEPTH // 2
EPS = 1e-6

WA = N_HEADS_A * HEAD_DIM_A
KB = N_HEADS_B * HEAD_K_B
VB = N_HEADS_B * HEAD_V_B
P_AB = 3 * WA + 2 * KB + 2 * VB + GATE_RANK

kernel_name = "chunk_band_gla_conformer_hybrid_step"

def rms_norm(x, g):
    xf = x.astype(jnp.float32)
    y = xf * lax.rsqrt(jnp.mean(xf * xf, axis=-1, keepdims=True) + EPS)
    return (y * g.astype(jnp.float32)).astype(x.dtype)

def layer_norm(x, g, b):
    xf = x.astype(jnp.float32)
    mu = jnp.mean(xf, axis=-1, keepdims=True)
    var = jnp.mean(jnp.square(xf - mu), axis=-1, keepdims=True)
    y = (xf - mu) * lax.rsqrt(var + EPS)
    return (y * g.astype(jnp.float32) + b.astype(jnp.float32)).astype(x.dtype)

def ab_project(xn, w_in, q_g, k_g, gate_w, gate_b):
    B, T, _ = xn.shape
    h = xn @ w_in
    o = np.cumsum([0, WA, WA, WA, KB, KB, VB, VB, GATE_RANK])
    qa, ka, va, qb, kb, vb, gb, lr = [h[..., o[n]:o[n + 1]] for n in range(8)]
    qa = rms_norm(qa.reshape(B, T, N_HEADS_A, HEAD_DIM_A), q_g)
    ka = rms_norm(ka.reshape(B, T, N_HEADS_A, HEAD_DIM_A), k_g)
    va = va.reshape(B, T, N_HEADS_A, HEAD_DIM_A)
    qb = qb.reshape(B, T, N_HEADS_B, HEAD_K_B) * (HEAD_K_B ** -0.5)
    kb = kb.reshape(B, T, N_HEADS_B, HEAD_K_B)
    vb = vb.reshape(B, T, N_HEADS_B, HEAD_V_B)
    gb = gb.reshape(B, T, N_HEADS_B, HEAD_V_B)
    logit = (lr @ gate_w + gate_b).astype(jnp.float32)
    la = (jax.nn.log_sigmoid(logit) / GATE_NORM).reshape(B, T, N_HEADS_B, HEAD_K_B)
    return qa, ka, va, qb, kb, vb, gb, la

def rel_bias(table, dist):
    idx = jnp.clip(dist, REL_MIN, REL_MAX) - REL_MIN
    return table[:, idx]

def attend(q, k, v, bias, valid=None):
    s = jnp.einsum('bqhd,bkhd->bhqk', q, k).astype(jnp.float32) * (HEAD_DIM_A ** -0.5)
    s = s + bias.astype(jnp.float32)[None]
    if valid is not None:
        s = jnp.where(valid, s, -1e30)
    p = jax.nn.softmax(s, axis=-1).astype(v.dtype)
    return jnp.einsum('bhqk,bkhd->bqhd', p, v)

def band_attn_prompt(q, k, v, table):
    B, S, H, dh = q.shape
    nc = S // CHUNK
    pad = A_PAST_CHUNKS * CHUNK
    band = pad + CHUNK
    kp = jnp.pad(k, ((0, 0), (pad, 0), (0, 0), (0, 0)))
    vp = jnp.pad(v, ((0, 0), (pad, 0), (0, 0), (0, 0)))
    qc = q.reshape(B, nc, CHUNK, H, dh).swapaxes(0, 1)
    r = jnp.arange(band)
    i = jnp.arange(CHUNK)
    bias = rel_bias(table, (pad + i)[:, None] - r[None, :])

    def one_chunk(args):
        c, qb = args
        kb = lax.dynamic_slice_in_dim(kp, c * CHUNK, band, axis=1)
        vb = lax.dynamic_slice_in_dim(vp, c * CHUNK, band, axis=1)
        valid = (c * CHUNK - pad + r) >= 0
        return attend(qb, kb, vb, bias, valid[None, None, None, :])

    out = lax.map(one_chunk, (jnp.arange(nc), qc))
    return out.swapaxes(0, 1).reshape(B, S, H, dh)

def band_attn_sample(q, k_new, v_new, ck, cv, table):
    T = q.shape[1]
    Lc = ck.shape[1]
    kk = jnp.concatenate([ck.astype(k_new.dtype), k_new], axis=1)
    vv = jnp.concatenate([cv.astype(v_new.dtype), v_new], axis=1)
    qpos = PAST_LEN + jnp.arange(T)
    kpos = jnp.concatenate([PAST_LEN - Lc + jnp.arange(Lc), PAST_LEN + jnp.arange(T)])
    bias = rel_bias(table, qpos[:, None] - kpos[None, :])
    return attend(q, kk, vv, bias)

def gla_chunk(S, inp):
    q, k, v, la = inp
    q = q.astype(jnp.float32)
    k = k.astype(jnp.float32)
    v = v.astype(jnp.float32)
    T = q.shape[1]
    b = jnp.cumsum(la, axis=1)
    causal = jnp.tril(jnp.ones((T, T), dtype=bool))
    diff = b[:, :, None] - b[:, None, :]
    decay = jnp.exp(jnp.where(causal[None, :, :, None, None], diff, -jnp.inf))
    attn = jnp.einsum('bihd,bjhd,bijhd->bhij', q, k, decay)
    o = jnp.einsum('bhij,bjhv->bihv', attn, v) + jnp.einsum('bihd,bhdv->bihv', q * jnp.exp(b), S)
    b_last = b[:, -1]
    S_new = jnp.exp(b_last)[..., None] * S + jnp.einsum(
        'bjhd,bjhv->bhdv', k * jnp.exp(b_last[:, None] - b), v)
    return S_new, o

def gla_prompt(q, k, v, la):
    B, S, H, dk = q.shape
    nc = S // CHUNK

    def to_chunks(a):
        return a.reshape(B, nc, CHUNK, H, a.shape[-1]).swapaxes(0, 1)

    S0 = jnp.zeros((B, H, dk, HEAD_V_B), jnp.float32)
    S_fin, o = lax.scan(gla_chunk, S0, (to_chunks(q), to_chunks(k), to_chunks(v), to_chunks(la)))
    return o.swapaxes(0, 1).reshape(B, S, H, HEAD_V_B), S_fin

def ab_merge(oa, ob, gb, onorm_g, w_out):
    B, T = oa.shape[:2]
    ob = rms_norm(ob.astype(gb.dtype), onorm_g) * jax.nn.silu(gb)
    cat = jnp.concatenate([oa.reshape(B, T, WA), ob.reshape(B, T, VB).astype(oa.dtype)], axis=-1)
    return cat @ w_out

def conv_module(xn, buf, w1, b1, w_dw, b_dw, ln_g, ln_b, w2, b2):
    u = xn @ w1 + b1
    u = u[..., :D_MODEL] * jax.nn.sigmoid(u[..., D_MODEL:])
    full = jnp.concatenate([buf.astype(u.dtype), u], axis=1)
    y = lax.conv_general_dilated(full, w_dw.astype(full.dtype)[:, None, :], window_strides=(1,),
                                 padding='VALID', dimension_numbers=('NWC', 'WIO', 'NWC'),
                                 feature_group_count=D_MODEL) + b_dw
    y = jax.nn.silu(layer_norm(y, ln_g, ln_b))
    return y @ w2 + b2, full[:, -(CONV_W - 1):]

def ffn(xn, w_up, w_down):
    return jnp.square(jax.nn.relu(xn @ w_up)) @ w_down

def setup_inputs(seed: int = 0) -> dict:
    key = jax.random.key(seed)
    ks = jax.random.split(key, 32)

    def nrm(k, shape, scale):
        return jax.random.normal(k, shape, jnp.float32) * scale

    la_len = min(A_PAST_CHUNKS * CHUNK, PAST_LEN)
    return {
        "x_prompt": nrm(ks[0], (BATCH, SEQ, D_MODEL), 1.0),
        "x_sample": nrm(ks[1], (DEC_BATCH, DEC_SEQ, D_MODEL), 1.0),
        "cache_a_k": nrm(ks[2], (N_AB_LAYERS, DEC_BATCH, la_len, N_HEADS_A, HEAD_DIM_A), 1.0),
        "cache_a_v": nrm(ks[3], (N_AB_LAYERS, DEC_BATCH, la_len, N_HEADS_A, HEAD_DIM_A), 1.0),
        "state_b": nrm(ks[4], (N_AB_LAYERS, DEC_BATCH, N_HEADS_B, HEAD_K_B, HEAD_V_B), 0.5),
        "cache_c": nrm(ks[5], (N_C_LAYERS, DEC_BATCH, CONV_W - 1, D_MODEL), 0.5),
        "norm_mix_g": 1.0 + nrm(ks[6], (DEPTH, D_MODEL), 0.02),
        "norm_ffn_g": 1.0 + nrm(ks[7], (DEPTH, D_MODEL), 0.02),
        "w_in_ab": nrm(ks[8], (N_AB_LAYERS, D_MODEL, P_AB), D_MODEL ** -0.5),
        "a_q_norm_g": 1.0 + nrm(ks[9], (N_AB_LAYERS, HEAD_DIM_A), 0.02),
        "a_k_norm_g": 1.0 + nrm(ks[10], (N_AB_LAYERS, HEAD_DIM_A), 0.02),
        "a_rel_bias": nrm(ks[11], (N_AB_LAYERS, N_HEADS_A, N_REL), 0.5),
        "b_gate_w_up": nrm(ks[12], (N_AB_LAYERS, GATE_RANK, KB), GATE_RANK ** -0.5),
        "b_gate_b": nrm(ks[13], (N_AB_LAYERS, KB), 0.1),
        "b_out_norm_g": 1.0 + nrm(ks[14], (N_AB_LAYERS, HEAD_V_B), 0.02),
        "w_out_ab": nrm(ks[15], (N_AB_LAYERS, D_MODEL, D_MODEL), D_MODEL ** -0.5),
        "c_w_pw1": nrm(ks[16], (N_C_LAYERS, D_MODEL, 2 * D_MODEL), D_MODEL ** -0.5),
        "c_b_pw1": nrm(ks[17], (N_C_LAYERS, 2 * D_MODEL), 0.02),
        "c_w_dw": nrm(ks[18], (N_C_LAYERS, CONV_W, D_MODEL), CONV_W ** -0.5),
        "c_b_dw": nrm(ks[19], (N_C_LAYERS, D_MODEL), 0.02),
        "c_ln_g": 1.0 + nrm(ks[20], (N_C_LAYERS, D_MODEL), 0.02),
        "c_ln_b": nrm(ks[21], (N_C_LAYERS, D_MODEL), 0.02),
        "c_w_pw2": nrm(ks[22], (N_C_LAYERS, D_MODEL, D_MODEL), D_MODEL ** -0.5),
        "c_b_pw2": nrm(ks[23], (N_C_LAYERS, D_MODEL), 0.02),
        "w_ffn_up": nrm(ks[24], (DEPTH, D_MODEL, D_FF), D_MODEL ** -0.5),
        "w_ffn_down": nrm(ks[25], (DEPTH, D_FF, D_MODEL), D_FF ** -0.5),
    }

def reference(x_prompt, x_sample, cache_a_k, cache_a_v, state_b, cache_c,
              norm_mix_g, norm_ffn_g, w_in_ab, a_q_norm_g, a_k_norm_g, a_rel_bias,
              b_gate_w_up, b_gate_b, b_out_norm_g, w_out_ab,
              c_w_pw1, c_b_pw1, c_w_dw, c_b_dw, c_ln_g, c_ln_b, c_w_pw2, c_b_pw2,
              w_ffn_up, w_ffn_down):
    xp, xs = x_prompt, x_sample
    akp, avp, aks, avs, sbp, sbs, ccp, ccs = [], [], [], [], [], [], [], []
    for l in range(DEPTH):
        hp = rms_norm(xp, norm_mix_g[l])
        hs = rms_norm(xs, norm_mix_g[l])
        if l % 2 == 0:
            i = l // 2
            proj = (w_in_ab[i], a_q_norm_g[i], a_k_norm_g[i], b_gate_w_up[i], b_gate_b[i])
            qa, ka, va, qb, kb, vb, gb, la = ab_project(hp, *proj)
            oa = band_attn_prompt(qa, ka, va, a_rel_bias[i])
            ob, sb = gla_prompt(qb, kb, vb, la)
            mp = ab_merge(oa, ob, gb, b_out_norm_g[i], w_out_ab[i])
            lp = min(A_PAST_CHUNKS * CHUNK, xp.shape[1])
            akp.append(ka[:, -lp:])
            avp.append(va[:, -lp:])
            sbp.append(sb)
            qa, ka, va, qb, kb, vb, gb, la = ab_project(hs, *proj)
            oa = band_attn_sample(qa, ka, va, cache_a_k[i], cache_a_v[i], a_rel_bias[i])
            sb, ob = gla_chunk(state_b[i].astype(jnp.float32), (qb, kb, vb, la))
            ms = ab_merge(oa, ob, gb, b_out_norm_g[i], w_out_ab[i])
            aks.append(ka)
            avs.append(va)
            sbs.append(sb)
        else:
            j = l // 2
            cp = (c_w_pw1[j], c_b_pw1[j], c_w_dw[j], c_b_dw[j], c_ln_g[j], c_ln_b[j],
                  c_w_pw2[j], c_b_pw2[j])
            zero_buf = jnp.zeros((xp.shape[0], CONV_W - 1, D_MODEL), hp.dtype)
            mp, bp = conv_module(hp, zero_buf, *cp)
            ms, bs = conv_module(hs, cache_c[j], *cp)
            ccp.append(bp)
            ccs.append(bs)
        xp = xp + mp.astype(xp.dtype)
        xs = xs + ms.astype(xs.dtype)
        xp = xp + ffn(rms_norm(xp, norm_ffn_g[l]), w_ffn_up[l], w_ffn_down[l]).astype(xp.dtype)
        xs = xs + ffn(rms_norm(xs, norm_ffn_g[l]), w_ffn_up[l], w_ffn_down[l]).astype(xs.dtype)
    return (xp, xs,
            jnp.stack(akp), jnp.stack(avp), jnp.stack(aks), jnp.stack(avs),
            jnp.stack(sbp), jnp.stack(sbs), jnp.stack(ccp), jnp.stack(ccs))


_drawn_inputs = setup_inputs


def setup_inputs(seed=0):
    import zlib

    import numpy as np

    out = dict(_drawn_inputs(seed))
    spreads = {}
    factors = {'a_q_norm_g': 111.813,
     'b_out_norm_g': 16.531,
     'c_b_dw': 3.75,
     'c_ln_g': 141.157,
     'c_ln_b': 126.556,
     'c_b_pw2': 96.759,
     'norm_ffn_g': 5.043,
     'a_rel_bias': 4.889}
    for name, (base, spread) in spreads.items():
        noise = np.random.default_rng([zlib.crc32(name.encode()), seed]).standard_normal(out[name].shape)
        drawn = base * np.exp(spread * noise) if base else spread * noise
        out[name] = __import__('jax').numpy.asarray(drawn.astype(out[name].dtype))
    for name, factor in factors.items():
        out[name] = (out[name] * factor).astype(out[name].dtype)
    return out
```

```python
from contextlib import ExitStack

import concourse.bass as bass
from concourse import mybir

F32 = mybir.dt.float32
F32R = mybir.dt.float32r
ACT = mybir.ActivationFunctionType
ALU = mybir.AluOpType
AX = mybir.AxisListType

P = 128
D = 1024
KT = D // P
SEQ, DEC = 512, 32
TOK = SEQ + DEC
HALF = TOK // 2
TT = SEQ // P
NF = 4 * D // D
CHUNK = 64
HA, DA = 8, 64
HB, DKB, DVB = 4, 64, 128
PAST = 256
NREL = 192
RANK = 16
CONV = 31
PAD = CONV - 1
CW = SEQ + PAD + DEC + 2
PE_TAPS = 10
FW = PAD + CW
EPS = 1e-6
NEG = -1e30

U_IN, U_OUT, U_FFN0 = 0, 12, 16
U_PW1 = U_FFN0 + 8 * NF
U_PW2 = U_PW1 + 8
U_FFN1 = U_PW2 + 4
U_END = U_FFN1 + 8 * NF
FFN_ORDER = [("up", 0)] + [s for c in range(1, NF) for s in (("up", c), ("down", c - 1))] + [("down", NF - 1)]

X_MIX0, X_CAT, X_FFN0, X_MIX1, X_PW2, X_FFN1 = (8 * n for n in range(6))

V_MIX, V_FFN, V_B1, V_BDW, V_LNG, V_LNB, V_B2, V_GB, V_ON, V_QG, V_KG = 0, 16, 32, 48, 56, 64, 72, 80, 82, 83, 84
V_N = 85

T_Q, T_K, T_V, T_QB, T_KB, T_VB, T_GB = 0, 4, 8, 12, 14, 16, 20
N_PROJ = 24


def tile0(u):
    return 8 + 2 * u + (2 if u >= U_PW2 else 0)


def levels():
    return [64 >> n for n in range(7)]


def hybrid_kernel(nc, x_prompt, x_sample, cache_a_k, cache_a_v, state_b, cache_c, norm_mix_g, norm_ffn_g,
                  w_in_ab, a_q_norm_g, a_k_norm_g, a_rel_bias, b_gate_w_up, b_gate_b, b_out_norm_g, w_out_ab,
                  c_w_pw1, c_b_pw1, c_w_dw, c_b_dw, c_ln_g, c_ln_b, c_w_pw2, c_b_pw2, w_ffn_up, w_ffn_down,
                  y_prompt, y_sample, ak_prompt, av_prompt, ak_sample, av_sample, sb_prompt, sb_sample,
                  cc_prompt, cc_sample):
    ctx = ExitStack()

    def sb(stack, name, shape, dt=F32):
        return stack.enter_context(nc.sbuf_tensor(name, shape, dt))

    def sem(name):
        return ctx.enter_context(nc.semaphore(name))

    resid = sb(ctx, "resid", [P, KT, TOK])
    w_raw = sb(ctx, "w_raw", [P, 2, KT, 256])
    w_h = sb(ctx, "w_h", [P, 2, KT, 256], F32R)
    w_l = sb(ctx, "w_l", [P, 2, KT, 256], F32R)
    ident = sb(ctx, "ident", [P, P])
    ones = sb(ctx, "ones", [P, P])
    mean_d = sb(ctx, "mean_d", [P, P])
    mean_ha = sb(ctx, "mean_ha", [P, P])
    mean_hb = sb(ctx, "mean_hb", [P, P])
    masks = sb(ctx, "masks", [P, 8, P])
    vec_rows = sb(ctx, "vec_rows", [V_N, P])
    vecs = sb(ctx, "vecs", [P, V_N])
    g_qk = sb(ctx, "g_qk", [P, 8])
    eps = sb(ctx, "eps", [P, 1])
    w_dw = sb(ctx, "w_dw", [P, KT, CONV])
    w_dw_h = sb(ctx, "w_dw_h", [P, KT, PE_TAPS], F32R)
    w_dw_l = sb(ctx, "w_dw_l", [P, KT, PE_TAPS])
    cc_T = sb(ctx, "cc_T", [P, KT, PAD])
    gate_w = sb(ctx, "gate_w", [RANK, HB * DKB])
    state = sb(ctx, "state", [P, 2, DVB])
    state_s = sb(ctx, "state_s", [P, 2, DVB])
    sq = sb(ctx, "sq", [P, 2, CW])
    sumsq = sb(ctx, "sumsq", [P, TOK])
    rstd = sb(ctx, "rstd", [P, CW])
    xn = sb(ctx, "xn", [P, 3, TOK])
    small = sb(ctx, "small", [P, 16])

    with ExitStack() as over:
        x_h = sb(over, "x_h", [P, KT, TOK], F32R)
        x_l = sb(over, "x_l", [P, KT, TOK], F32R)
        hid_h = [sb(over, f"hid_h{n}", [P, KT, TOK], F32R) for n in range(2)]
        hid_l = [sb(over, f"hid_l{n}", [P, KT, TOK], F32R) for n in range(2)]
        relu = sb(over, "relu", [P, 2, TOK])
        relu2 = sb(over, "relu2", [P, 2, TOK])
    with ExitStack() as over:
        x_rows = sb(over, "x_rows", [P, TT + 1, D])
        dw_rows = sb(over, "dw_rows", [CONV, D])
        cc_rows = sb(over, "cc_rows", [PAD, D])
    with ExitStack() as over:
        v_rows = sb(over, "v_rows", [P, TT + 1, HA * DA])
        vb_rows = sb(over, "vb_rows", [P, TT + 1, HB * DVB])
        with ExitStack() as att:
            k_rows = sb(att, "k_rows", [P, TT + 1, HA * DA])
            ck_T = sb(att, "ck_T", [P, 4, PAST])
        kd = sb(over, "kd", [P, 2, TOK])
        qe = sb(over, "qe", [P, 2, TOK])
        kd_rows = sb(over, "kd_rows", [P, TT + 1, HB * DKB])
    with ExitStack() as over:
        masked = sb(over, "masked", [P, 2, 8, P])
        pair = sb(over, "pair", [P, 2, P])
    with ExitStack() as over:
        sb(over, "under_x", [P, 2, KT, TOK])
        with ExitStack() as mix:
            proj = sb(mix, "proj", [P, N_PROJ, TOK])
            lr = sb(mix, "lr", [RANK, TOK])
            with ExitStack() as part:
                qk_sq = sb(part, "qk_sq", [P, 8, TOK])
                wlr = sb(part, "wlr", [P, KT, RANK])
                wlr_h = sb(part, "wlr_h", [P, KT, P], F32R)
                wlr_l = sb(part, "wlr_l", [P, KT, P], F32R)
            with ExitStack() as part:
                ck_rows = sb(part, "ck_rows", [P, 2, HA * DA])
                cv_rows = sb(part, "cv_rows", [P, 2, HA * DA])
                bias = sb(part, "bias", [P, 2, 512])
                prob = sb(part, "prob", [P, 3, 512])
                prob_T = sb(part, "prob_T", [P, 2, 512])
                gl_a = sb(part, "gl_a", [P, TOK])
                gl_b = sb(part, "gl_b", [P, TOK])
            with ExitStack() as part:
                lev = sb(part, "lev", [P, 7, TOK])
            rel = sb(mix, "rel", [HA, NREL])
            rel_u = sb(mix, "rel_u", [HA, 1, 640])
        with ExitStack() as mix:
            glu = sb(mix, "glu", [P, KT, FW])
            cv = sb(mix, "cv", [P, KT, CW])
            sig = sb(mix, "sig", [P, 2, TOK])
            glu_h = sb(mix, "glu_h", [P, 2, FW], F32R)
            glu_l = sb(mix, "glu_l", [P, 2, FW], F32R)
            with ExitStack() as part:
                diag_h = sb(part, "diag_h", [P, 2, PE_TAPS, P], F32R)
                diag_l = sb(part, "diag_l", [P, 2, PE_TAPS, P], F32R)
            ccn = sb(mix, "ccn", [PAD, 2, D])
        y_rows = sb(over, "y_rows", [P, 2, TT + 1, P])
        y_fin = sb(over, "y_fin", [P, 2, TOK])
    bt = proj[:, T_V:T_V + 2, :]
    eb = proj[:, T_V + 2:T_V + 4, :]
    ps = ctx.enter_context(nc.psum_tensor("ps", [P, 8, 512], F32))
    rel_dram = nc.dram_tensor("rel_scratch", (HA, P, 640), F32, kind="Internal").ap()

    def slot(m):
        return ps[:, 2 * m:2 * m + 2, 0:HALF]

    def flat(m):
        return ps[:, 2 * m:2 * m + 2, :].rearrange("p a b -> p (a b)")

    def halves(ap):
        return ap.rearrange("p (a t) -> p a t", a=2)

    def sum_ps(n, w=HALF):
        return ps[:, 4 + 2 * n:6 + 2 * n, 0:w]

    def frames(c):
        return slice(c * P, c * P + (P if c < TT else DEC))

    def width(c):
        return P if c < TT else DEC

    x_landed = [sem(f"x_landed{c}") for c in range(TT + 1)]
    rows_landed = sem("rows_landed")
    late_landed = sem("late_landed")
    w_landed = [sem("w_landed0"), sem("w_landed1")]
    w_hi, w_lo = sem("w_hi"), sem("w_lo")
    consts = sem("consts")
    vec_T = sem("vec_T")
    vec_ready = sem("vec_ready")
    gemm_done = sem("gemm_done")
    slot_free = [sem("slot_free0"), sem("slot_free1")]
    sq_ready, sumsq_step, ms_ready, std_ready, rstd_ready = (sem(n) for n in (
        "sq_ready", "sumsq_step", "ms_ready", "std_ready", "rstd_ready"))
    xn_ready, xh_ready, xl_ready = sem("xn_ready"), sem("xh_ready"), sem("xl_ready")
    relu2_done, hidh_done, hidl_done = sem("relu2_done"), sem("hidh_done"), sem("hidl_done")
    wlr_hi, wlr_lo = sem("wlr_hi"), sem("wlr_lo")
    qk_sq_a, qk_sq_v, qk_ms, qk_std, qk_norm = (sem(n) for n in ("qk_sq_a", "qk_sq_v", "qk_ms", "qk_std", "qk_norm"))
    rel_built, rel_stored, bias_landed, bias_ready = (sem(n) for n in (
        "rel_built", "rel_stored", "bias_landed", "bias_ready"))
    lr_done, lr_ready, gate_done, gate_abs, gate_min, gate_ln, bt_ready, eb_ready = (sem(n) for n in (
        "lr_done", "lr_ready", "gate_done", "gate_abs", "gate_min", "gate_ln", "bt_ready", "eb_ready"))
    rows_T = sem("rows_T")
    rows_out = [sem("rows_out_a"), sem("rows_out_v")]
    silu_done = sem("silu_done")
    score_done, score_read, nmax_ready, exp_done, prob_ready, probT_done, probT_ready, o_done, o_copied = (
        sem(n) for n in ("score_done", "score_read", "nmax_ready", "exp_done", "prob_ready", "probT_done",
                         "probT_ready", "o_done", "o_copied"))
    lev_diff, lev_exp, lev_ready, kd_diff, kd_exp, kd_ready, kd_T, kd_rows_ready = (sem(n) for n in (
        "lev_diff", "lev_exp", "lev_ready", "kd_diff", "kd_exp", "kd_ready", "kd_T", "kd_rows_ready"))
    pairs_done, masked_done, pair_ready, kv_done, state_ready, ob_done, ob_ready = (sem(n) for n in (
        "pairs_done", "masked_done", "pair_ready", "kv_done", "state_ready", "ob_done", "ob_ready"))
    ob_sq, ob_ms, ob_std, ob_cat = (sem(n) for n in ("ob_sq", "ob_ms", "ob_std", "ob_cat"))
    w_dw_hi, w_dw_lo, glu_hi, glu_lo, diag_ready, taps_done = (
        sem(n) for n in ("w_dw_hi", "w_dw_lo", "glu_hi", "glu_lo", "diag_ready", "taps_done"))
    glu_edges, conv_step, conv_ready, cvmean, cv_centred, cv_sq, cv_var, cv_std, cv_norm, cv_silu = (
        sem(n) for n in ("glu_edges", "conv_step", "conv_ready", "cvmean", "cv_centred", "cv_sq",
                         "cv_var", "cv_std", "cv_norm", "cv_silu"))
    y_ready, y_T, y_stage = sem("y_ready"), sem("y_T"), sem("y_stage")
    y_stored = [sem("y_stored0"), sem("y_stored1")]
    a_step, v_step, p_step = sem("a_step"), sem("v_step"), sem("p_step")
    stored = sem("stored")

    def sum_flat(n):
        return ps[:, 4 + 2 * n:6 + 2 * n, :].rearrange("p a b -> p (a b)")

    def keys(n):
        return (n % 5 + 1) * P if n % 5 < TT else PAST + DEC

    def kd_bank(n):
        return 6 - 2 * n

    def rows_group(g):
        if g < 15:
            c, kind = g // 3, g % 3
            M = width(c)
            return (k_rows, v_rows, vb_rows)[kind][0:M, c, :], ps[0:M, g % 4, :]
        q = g - 15
        return ck_T[:, 2 * q:2 * q + 2, :].rearrange("p a t -> p (a t)"), ps[:, g % 4, :]

    def ob_root(act, h):
        act.wait_ge(ob_ms, h + 1)
        if h >= 1:
            act.wait_ge(ob_cat, h)
        act.activation(halves(sumsq[:]), sum_ps(h % 2), ACT.Sqrt, bias=eps[:, 0:1]).then_inc(ob_std, 1)

    block = ctx.enter_context(nc.Block())

    def w_view(w):
        return w.rearrange("(k p) n -> p k n", p=P)

    @block.sync
    def _(sp):
        xp = x_prompt[0].rearrange("(c p) d -> c p d", p=P)
        for c in range(TT):
            sp.dma_start(x_rows[:, c, :], xp[c]).then_inc(x_landed[c], 16)
        sp.dma_start(x_rows[0:DEC, TT, :], x_sample[0]).then_inc(x_landed[TT], 16)

        def stream(u0, units, source, first=False):
            if first:
                for s in range(2):
                    sp.dma_start(w_raw[:, s], source(s)).then_inc(w_landed[s], 16)
            with sp.Fori(1 if first else 0, units // 2) as i:
                for s in range(2):
                    sp.wait_ge(w_lo, i * 2 + (u0 + s - 1))
                    sp.dma_start(w_raw[:, s], source(i * 2 + s)).then_inc(w_landed[s], 16)

        def columns(w, at=0):
            v = w_view(w)
            return lambda n: v[:, :, bass.ds(n * 256 + at, 256)]

        def ffn(layer, u0):
            for n, (way, c) in enumerate(FFN_ORDER):
                src = (columns(w_ffn_up[layer], c * D) if way == "up"
                       else columns(w_ffn_down[layer][c * D:(c + 1) * D, :]))
                stream(u0 + 4 * n, 4, src)

        stream(U_IN, 12, columns(w_in_ab[0]), first=True)
        stream(U_OUT, 4, columns(w_out_ab[0]))
        ffn(0, U_FFN0)
        stream(U_PW1, 8, columns(c_w_pw1[0]))
        stream(U_PW2, 4, columns(c_w_pw2[0]))
        ffn(1, U_FFN1)
        yp = y_prompt[0].rearrange("(c p) d -> p c d", p=P)
        for k in range(KT):
            sp.wait_ge(y_stage, 2 * (k + 1))
            sp.dma_start(yp[:, :, k * P:(k + 1) * P], y_rows[:, k % 2, 0:TT, :]).then_inc(y_stored[k % 2], 16)
            sp.dma_start(y_sample[0][:, k * P:(k + 1) * P], y_rows[0:DEC, k % 2, TT, :])\
                .then_inc(y_stored[k % 2], 16)
        for n in range(2):
            sp.wait_ge(y_stored[n], 32 * (KT // 2))

    @block.gpsimd
    def _(pool):
        steps = [0]

        def own(ins):
            ins.then_inc(p_step, 1)
            steps[0] += 1
            pool.wait_ge(p_step, steps[0])

        pool.memset(ones[:], 1.0)
        pool.memset(mean_d[:], 1.0 / D)
        pool.memset(mean_hb[:], 1.0 / DVB)
        pool.memset(eps[:], EPS)
        pool.memset(wlr_h[:].bitcast(F32), 0.0)
        pool.memset(wlr_l[:].bitcast(F32), 0.0)
        pool.memset(mean_ha[:], 0.0)
        own(pool.memset(ident[:], 0.0))
        own(pool.affine_select(out=ident[:], in_=ident[:], compare_op=ALU.not_equal, fill=1.0, base=0,
                               pattern=[[-1, P]], channel_multiplier=1))
        own(pool.memset(mean_ha[0:DA, 0:DA], 1.0 / DA))
        pool.memset(mean_ha[DA:P, DA:P], 1.0 / DA).then_inc(consts, 1)
        pool.wait_ge(consts, 1)
        own(pool.memset(masks[:], 0.0))
        for n, s in enumerate(levels()):
            second = masks[:, n, :].rearrange("p (a h c) -> p a h c", h=2, c=s)[:, :, 1, :]
            na = P // (2 * s)
            own(pool.memset(second, DKB ** -0.5))
            own(pool.affine_select(out=second, in_=second, compare_op=ALU.is_ge, fill=0.0, base=0,
                                   pattern=[[-2 * s, na], [0, s]], channel_multiplier=1))
            own(pool.affine_select(out=second, in_=second, compare_op=ALU.is_ge, fill=0.0, base=s - 1,
                                   pattern=[[2 * s, na], [0, s]], channel_multiplier=-1))
        pool.affine_select(out=masks[:, 7, :], in_=masks[:, 7, :], compare_op=ALU.not_equal, fill=DKB ** -0.5,
                           base=0, pattern=[[-1, P]], channel_multiplier=1).then_inc(consts, 1)
        pool.wait_ge(rel_built, 3)
        pool.dma_start(rel_dram, rel_u[:].to_broadcast((HA, P, 640))).then_inc(rel_stored, 16)
        pool.wait_ge(rel_stored, 16)

        def sum_squares(n, k, parity, first):
            pool.wait_ge(sq_ready, k + (8 * n + 1))
            if first:
                pool.tensor_copy(sumsq[:], sq[:, parity, 0:TOK]).then_inc(sumsq_step, 1)
            else:
                pool.wait_ge(sumsq_step, k + 8 * n)
                pool.tensor_tensor(sumsq[:], sumsq[:], sq[:, parity, 0:TOK], ALU.add).then_inc(sumsq_step, 1)

        def sum_all(n):
            sum_squares(n, 0, 0, True)
            for k in range(1, 4):
                sum_squares(n, k, k % 2, False)
            with pool.Fori(1, KT // 4) as i:
                for q in range(4):
                    sum_squares(n, i * 4 + q, q % 2, False)

        for k in range(KT):
            sum_squares(0, k, k % 2, k == 0)

        pool.wait_ge(qk_norm, 10)
        pool.wait_ge(lr_done, 1)
        pool.dma_start(ck_rows[:], cache_a_k[0, 0].rearrange("(a p) h d -> p a (h d)", p=P)).then_inc(late_landed, 16)
        pool.dma_start(cv_rows[:], cache_a_v[0, 0].rearrange("(a p) h d -> p a (h d)", p=P)).then_inc(late_landed, 16)

        def load_bias(h):
            src = bass.AP(tensor=rel_dram.tensor, offset=h * P * 640 + P - 1, ap=[[640 - 1, P], [1, 512]])
            pool.dma_start(bias[:, h % 2, :], src).then_inc(bias_landed, 16)
            pool.wait_ge(bias_landed, 16 * (h + 1))
            pool.memset(bias[0:CHUNK, h % 2, 512 - CHUNK:512], NEG).then_inc(bias_ready, 1)

        load_bias(0)
        load_bias(1)
        pool.wait_ge(rows_out[0], 8)
        pool.wait_ge(rows_out[1], 7)
        for rows, prompt, sample in ((k_rows, ak_prompt, ak_sample), (v_rows, av_prompt, av_sample)):
            pool.dma_start(prompt[0, 0].rearrange("(c p) h d -> p c (h d)", p=P), rows[:, 0:TT, :])\
                .then_inc(stored, 16)
            pool.dma_start(sample[0, 0].rearrange("t h d -> t (h d)"), rows[0:DEC, TT, :]).then_inc(stored, 16)
        for h in range(2, HA):
            pool.wait_ge(score_read, 5 * (h - 1))
            load_bias(h)
        pool.wait_ge(state_ready, 20)
        pool.dma_start(sb_prompt[0, 0].rearrange("(a b) k v -> (b k) a v", b=2), state[:]).then_inc(stored, 16)
        pool.dma_start(sb_sample[0, 0].rearrange("(a b) k v -> (b k) a v", b=2), state_s[:]).then_inc(stored, 16)

        sum_all(1)
        sum_all(2)
        pool.wait_ge(gemm_done, tile0(U_PW1))
        pool.memset(glu[:, :, 0:PAD], 0.0).then_inc(glu_edges, 1)
        pool.tensor_copy(glu[:, :, PAD + SEQ:PAD + SEQ + PAD], cc_T[:]).then_inc(glu_edges, 1)
        pool.memset(glu[:, :, FW - 2:FW], 0.0).then_inc(glu_edges, 1)
        pool.wait_ge(slot_free[0], tile0(U_PW2) // 2)
        pool.wait_ge(slot_free[1], tile0(U_PW2) // 2)
        pool.dma_start(cc_prompt[0, 0], ccn[:, 0, :]).then_inc(stored, 16)
        pool.dma_start(cc_sample[0, 0], ccn[:, 1, :]).then_inc(stored, 16)
        sum_all(3)
        pool.wait_ge(stored, 16 * 8)

    @block.scalar
    def _(act):
        steps = [0]

        def own(ins):
            ins.then_inc(a_step, 1)
            steps[0] += 1
            act.wait_ge(a_step, steps[0])

        rows = lambda v: v.rearrange("a (r p) -> (a r) p", p=P)
        for at, n, src in ((V_MIX, 16, rows(norm_mix_g)), (V_FFN, 16, rows(norm_ffn_g)), (V_B1, 16, rows(c_b_pw1)),
                           (V_BDW, 8, rows(c_b_dw)), (V_LNG, 8, rows(c_ln_g)), (V_LNB, 8, rows(c_ln_b)),
                           (V_B2, 8, rows(c_b_pw2)), (V_GB, 2, rows(b_gate_b)), (V_ON, 1, b_out_norm_g)):
            act.dma_start(vec_rows[at:at + n, :], src).then_inc(rows_landed, 16)
        for at, src in ((V_QG, a_q_norm_g), (V_KG, a_k_norm_g)):
            for b in range(2):
                act.dma_start(vec_rows[at:at + 1, b * DA:(b + 1) * DA], src).then_inc(rows_landed, 16)
        act.dma_start(wlr[:], w_view(w_in_ab[0])[:, :, N_PROJ * P:N_PROJ * P + RANK]).then_inc(rows_landed, 16)
        act.dma_start(dw_rows[:], c_w_dw[0]).then_inc(rows_landed, 16)
        act.dma_start(cc_rows[:], cache_c[0, 0]).then_inc(rows_landed, 16)
        act.dma_start(gate_w[:], b_gate_w_up[0]).then_inc(rows_landed, 16)
        act.dma_start(rel[:], a_rel_bias[0]).then_inc(rows_landed, 16)
        act.dma_start(state_s[:], state_b[0, 0].rearrange("(a b) k v -> (b k) a v", b=2)).then_inc(rows_landed, 16)

        def split_hi(u, i, d):
            s = d % 2
            act.wait_ge(w_landed[s], i * 16 + 16 * (u // 2 + d // 2 + 1))
            if not (u == 0 and isinstance(i, int) and i == 0 and d < 2):
                act.wait_ge(gemm_done, i * 2 * 2 + (tile0(u + d - 2) + 2))
            act.activation(w_h[:, s], w_raw[:, s], ACT.Copy).then_inc(w_hi, 1)

        def phase(u0, units, evacuate, last=False):
            with act.Fori(0, units // 2) as i:
                for s in range(2):
                    split_hi(u0, i, s + 1)
                    evacuate(i, s)

        def square(n, k, parity, ready, at):
            act.wait_ge(ready, at)
            if not (n == 0 and isinstance(k, int) and k < 2):
                act.wait_ge(sumsq_step, k + (8 * n - 1))
            act.activation(sq[:, parity, 0:TOK], resid_tile(k), ACT.Square).then_inc(sq_ready, 1)

        def resid_tile(k):
            return resid[:, k, :] if isinstance(k, int) else \
                resid[:, bass.ds(k, 1), :].rearrange("p o t -> p (o t)")

        act.wait_ge(rows_landed, 16 * 19)
        act.wait_ge(consts, 1)
        act.activation(wlr_h[:, :, 0:RANK], wlr[:], ACT.Copy).then_inc(wlr_hi, 1)
        for k in range(KT):
            square(0, k, k % 2, slot_free[k % 2], k // 2 + 1)
        split_hi(0, 0, 0)
        act.wait_ge(vec_ready, 1)
        act.activation(w_dw_h[:], w_dw[:, :, 0:PE_TAPS], ACT.Copy).then_inc(w_dw_hi, 1)

        def norm(n, x0):
            act.wait_ge(ms_ready, n + 1)
            act.activation(halves(sumsq[:]), sum_ps(0), ACT.Sqrt, bias=eps[:, 0:1]).then_inc(std_ready, 1)
            for k in range(KT):
                act.wait_ge(xn_ready, 8 * n + k + 1)
                act.activation(x_h[:, k, :], xn[:, k % 3, :], ACT.Copy).then_inc(xh_ready, 1)

        norm(0, X_MIX0)

        def proj_tile(t):
            return proj[:, bass.ds(t, 1), :].rearrange("p o (a t) -> p (o a) t", a=2)

        def evac_qk(i, s):
            act.wait_ge(gemm_done, i * 4 + (tile0(s) + 1))
            act.activation(proj_tile(i * 4 + 2 * s), slot(0), ACT.Copy)
            act.activation(qk_sq[:, bass.ds(i * 4 + 2 * s, 1), :].rearrange("p o (a t) -> p (o a) t", a=2),
                           slot(0), ACT.Square).then_inc(slot_free[0], 1)

        def evac_rest(i, s):
            act.wait_ge(gemm_done, i * 4 + (tile0(4 + s) + 1))
            act.activation(proj_tile(i * 4 + (8 + 2 * s)), slot(0), ACT.Copy).then_inc(slot_free[0], 1)
            act.wait_ge(qk_ms, i * 2 + (s + 1))
            act.wait_ge(qk_norm, i * 2 + (s + 2))
            act.activation(halves(sumsq[:]), sum_ps(s), ACT.Sqrt, bias=eps[:, 0:1]).then_inc(qk_std, 1)

        phase(0, 4, evac_qk)
        phase(4, 8, evac_rest)

        act.wait_ge(lr_done, 1)
        act.activation(halves(lr[:]), ps[0:RANK, 4:6, 0:HALF], ACT.Copy).then_inc(lr_ready, 1)
        act.wait_ge(slot_free[1], tile0(U_OUT) // 2)
        act.activation(proj[:, T_GB:T_GB + 4, :], proj[:, T_GB:T_GB + 4, :], ACT.Silu).then_inc(silu_done, 1)

        for g in range(0, 17, 2):
            act.wait_ge(rows_T, g + 1)
            dst, src = rows_group(g)
            act.activation(dst, src, ACT.Copy).then_inc(rows_out[0], 1)

        for n in range(2):
            act.wait_ge(gate_done, n + 1)
            if n:
                act.wait_ge(gate_ln, 2)
            own(act.activation(halves(gl_a[:]), sum_ps(n), ACT.Abs, bias=vecs[:, V_GB + n:V_GB + n + 1]))
            act.activation(gl_a[:], gl_a[:], ACT.Exp, scale=-1.0).then_inc(gate_abs, 1)
            act.wait_ge(gate_abs, n + 1)
            act.activation(gl_a[:], gl_a[:], ACT.Ln, bias=1.0).then_inc(gate_ln, 1)
            act.wait_ge(gate_ln, 2 * n + 2)
        for n in range(2):
            act.wait_ge(bt_ready, 5 * (n + 1))
            act.activation(eb[:, n, :], bt[:, n, :], ACT.Exp, scale=1.0 / 16).then_inc(eb_ready, 1)

        def exp_scores(n):
            M, nk = width(n % 5), keys(n)
            act.wait_ge(nmax_ready, n + 1)
            act.activation(prob[0:M, n % 3, 0:nk], prob[0:M, n % 3, 0:nk], ACT.Exp, bias=small[0:M, 4 + n % 3:5 + n % 3],
                           accum_out=small[0:M, 8 + n % 3:9 + n % 3]).then_inc(exp_done, 1)

        def copy_probT(n):
            M, nk = width(n % 5), keys(n)
            act.wait_ge(probT_done, n + 1)
            if n >= 2:
                act.wait_ge(o_done, n - 1)
            full = nk // P * M
            ins = act.activation(prob_T[:, n % 2, 0:full], ps[:, 2 + n % 2, 0:full], ACT.Copy)
            if nk % P:
                ins = act.activation(prob_T[0:nk % P, n % 2, full:full + M], ps[0:nk % P, 2 + n % 2, full:full + M],
                                     ACT.Copy)
            ins.then_inc(probT_ready, 1)

        def copy_o(n):
            h, c = n // 5, n % 5
            b = h % 2 * DA
            act.wait_ge(o_done, n + 1)
            act.activation(proj[b:b + DA, T_Q + h // 2, frames(c)], ps[b:b + DA, 4 + n % 2, 0:width(c)],
                           ACT.Copy).then_inc(o_copied, 1)

        for n in range(5 * HA + 2):
            if n < 5 * HA:
                exp_scores(n)
            if 1 <= n <= 5 * HA:
                copy_probT(n - 1)
            if n >= 2:
                copy_o(n - 2)

        for n in range(2):
            act.wait_ge(kd_diff, n + 1)
            act.activation(kd[:, n, :], kd[:, n, :], ACT.Exp, scale=1.0 / 16).then_inc(kd_exp, 1)
        for n in range(2):
            act.wait_ge(kd_T, n + 1)
            src = kd_bank(n)
            act.activation(kd_rows[:, 0:TT, n * P:(n + 1) * P], ps[:, src, :].rearrange("p (c f) -> p c f", f=P),
                           ACT.Copy)
            act.activation(kd_rows[0:DEC, TT, n * P:(n + 1) * P], ps[0:DEC, src + 1, 0:P], ACT.Copy)\
                .then_inc(kd_rows_ready, 1)
        for n in range(2):
            act.wait_ge(lev_diff, n + 1)
            act.activation(lev[:, 0:2, 0:SEQ], lev[:, 0:2, 0:SEQ], ACT.Exp, scale=1.0 / 16)
            act.activation(lev[:, 2:7, :], lev[:, 2:7, :], ACT.Exp, scale=1.0 / 16).then_inc(lev_exp, 1)
            for m in (range(9) if n == 0 else range(9, 20)):
                h, c = 2 * (m // 10) + m % 2, m % 10 // 2
                act.wait_ge(ob_done, m + 1)
                act.activation(proj[:, T_VB + h, frames(c)], ps[:, 4 + m % 2, 0:width(c)], ACT.Copy)\
                    .then_inc(ob_ready, 1)
        for h in range(HB):
            if h == 0:
                act.wait_ge(ob_ready, 20)
            if h >= 2:
                act.wait_ge(ob_ms, h - 1)
            act.activation(sq[:, h % 2, 0:TOK], proj[:, T_VB + h, :], ACT.Square).then_inc(ob_sq, 1)
            if h >= 1:
                ob_root(act, h - 1)
        ob_root(act, HB - 1)
        for k in range(KT):
            if k < 4:
                if k == 0:
                    act.wait_ge(ob_done, 20)
                    act.wait_ge(state_ready, 20)
                    act.wait_ge(stored, 16 * 4)
                src = proj[:, T_Q + k, :]
            else:
                act.wait_ge(ob_cat, k - 3)
                src = proj[:, T_VB + k - 4, :]
            act.activation(x_h[:, k, :], src, ACT.Copy).then_inc(xh_ready, 1)

        def squares_of(n, u0):
            def evacuate(i, s):
                for m in range(2):
                    square(n, i * 4 + (2 * s + m), m, slot_free[m], i * 2 + (tile0(u0 + s) // 2 + 1))
            return evacuate

        phase(U_OUT, 4, squares_of(1, U_OUT))
        norm(1, X_FFN0)

        def hidden(layer, c, u0):
            base = 4 * 8 * layer + 8 * c

            def evacuate(i, s):
                for m in range(2):
                    act.wait_ge(gemm_done, i * 4 + (tile0(u0 + s) + m + 1))
                    act.activation(halves(relu[:, m, :]), slot(m), ACT.Relu).then_inc(slot_free[m], 1)
                    act.wait_ge(relu2_done, i * 4 + (base + 2 * s + m + 1))
                    act.activation(hid_h[c % 2][:, bass.ds(i * 4 + (2 * s + m), 1), :].rearrange("p o t -> p (o t)"),
                                   relu2[:, m, :], ACT.Copy).then_inc(hidh_done, 1)
            return evacuate

        def ffn(layer, u0, last):
            for n, (way, c) in enumerate(FFN_ORDER):
                u = u0 + 4 * n
                if way == "up":
                    phase(u, 4, hidden(layer, c, u))
                elif c < NF - 1:
                    phase(u, 4, lambda i, s: None)
                else:
                    last(u)

        ffn(0, U_FFN0, lambda u: phase(u, 4, squares_of(2, u)))
        norm(2, X_MIX1)

        def gate(i, s):
            m = i * 2 + s
            act.wait_ge(taps_done, m + 1)
            for t in range(PE_TAPS):
                for part, w in ((diag_h, w_dw_h[:].bitcast(F32)), (diag_l, w_dw_l[:])):
                    w = w.rearrange("p k c -> p (k c)")
                    ins = act.activation(part[:, s, t, :], ident[:], ACT.Identity,
                                         scale=w[:, bass.ds(m * PE_TAPS + t, 1)])
            ins.then_inc(diag_ready, 1)
            act.wait_ge(gemm_done, i * 4 + (tile0(U_PW1 + s) + 1))
            act.activation(halves(sig[:, s, :]), slot(0), ACT.Sigmoid,
                           bias=vecs[:, bass.ds(i * 2 + (V_B1 + 8 + s), 1)]).then_inc(slot_free[0], 1)
            act.wait_ge(slot_free[1], m + (tile0(U_PW1) // 2 + 1))
            act.activation(glu_h[:, s, :], glu[:, bass.ds(m, 1), :].rearrange("p o t -> p (o t)"), ACT.Copy)\
                .then_inc(glu_hi, 1)

        act.wait_ge(w_dw_lo, 1)
        act.wait_ge(glu_edges, 3)
        phase(U_PW1, 8, gate)
        act.wait_ge(taps_done, KT + 2)
        act.wait_ge(gemm_done, tile0(U_PW2) - 1)
        act.activation(ccn[:, 0, :], flat(0)[0:PAD, :], ACT.Copy).then_inc(slot_free[0], 1)
        for k in range(KT):
            act.wait_ge(cv_centred, k + 1)
            if k >= 2:
                act.wait_ge(cv_var, k - 1)
            act.activation(sq[:, k % 2, :], cv[:, k, :], ACT.Square).then_inc(cv_sq, 1)
        act.wait_ge(cv_var, KT)
        act.activation(rstd[:].rearrange("p (a t) -> p a t", a=2), sum_ps(1, CW // 2), ACT.Sqrt,
                       bias=eps[:, 0:1]).then_inc(cv_std, 1)
        for k in range(KT):
            act.wait_ge(cv_norm, k + 1)
            if k >= 3:
                act.wait_ge(xl_ready, X_PW2 + k - 2)
            for to, of in ((slice(0, SEQ), slice(0, SEQ)), (slice(SEQ, TOK), slice(SEQ + PAD, SEQ + PAD + DEC))):
                ins = act.activation(xn[:, k % 3, to], cv[:, k, of], ACT.Silu, scale=vecs[:, V_LNG + k:V_LNG + k + 1],
                                     bias=vecs[:, V_LNB + k:V_LNB + k + 1])
            ins.then_inc(cv_silu, 1)
            act.wait_ge(cv_silu, k + 1)
            act.activation(x_h[:, k, :], xn[:, k % 3, :], ACT.Copy).then_inc(xh_ready, 1)
        phase(U_PW2, 4, squares_of(3, U_PW2))
        norm(3, X_FFN1)
        act.wait_ge(stored, 16 * 8)

        def y_out(u):
            for i in range(2):
                for s in range(2):
                    if u + 2 * i + s + 1 < U_END:
                        split_hi(u, i, s + 1)
                    for m in range(2):
                        k = 4 * i + 2 * s + m
                        act.wait_ge(y_T, k + 1)
                        if k >= 2:
                            act.wait_ge(y_stored[k % 2], 32 * (k // 2))
                        b = sum_flat(k % 2)
                        act.activation(y_rows[:, k % 2, 0:TT, :], b[:, 0:SEQ].rearrange("p (c f) -> p c f", f=P),
                                       ACT.Copy).then_inc(y_stage, 1)
                        act.activation(y_rows[0:DEC, k % 2, TT, :], b[0:DEC, 512:512 + P], ACT.Copy)\
                            .then_inc(y_stage, 1)

        ffn(1, U_FFN1, y_out)

    @block.tensor
    def _(pe):
        pe.wait_ge(rows_landed, 16 * 19)
        pe.wait_ge(consts, 1)
        pe.transpose(ps[:, 4, 0:V_N], vec_rows[:], ident[0:V_N, 0:V_N]).then_inc(vec_T, 1)
        for k in range(KT):
            ins = pe.transpose(ps[:, 5, k * CONV:(k + 1) * CONV], dw_rows[:, k * P:(k + 1) * P], ident[0:CONV, 0:CONV])
        ins.then_inc(vec_T, 1)
        for k in range(KT):
            ins = pe.transpose(ps[:, 6, k * PAD:(k + 1) * PAD], cc_rows[:, k * P:(k + 1) * P], ident[0:PAD, 0:PAD])
        ins.then_inc(vec_T, 1)
        for k in range(KT):
            if k >= 2:
                pe.wait_ge(slot_free[k % 2], k // 2)
            for c in range(TT + 1):
                if k == 0:
                    pe.wait_ge(x_landed[c], 16)
                M = width(c)
                ins = pe.transpose(flat(k % 2)[:, c * P:c * P + M], x_rows[0:M, c, k * P:(k + 1) * P],
                                   ident[0:M, 0:M])
            ins.then_inc(gemm_done, 1)

        def mean_of(dst, src, w, n=HALF, start=True, stop=True):
            for a in range(2):
                ins = pe.matmul(dst[:, a, :], w[:], src[:, a * n:(a + 1) * n], start=start, stop=stop)
            return ins

        def norm(n):
            pe.wait_ge(sumsq_step, 8 * (n + 1))
            mean_of(sum_ps(0), sumsq, mean_d).then_inc(ms_ready, 1)

        def tile(s, m, xh, xl, ready=None):
            for k in range(KT):
                if ready:
                    ready(k)
                w = slice(m * P, (m + 1) * P)
                for q, (a, b) in enumerate(((w_h, xh), (w_h, xl), (w_l, xh))):
                    for t in range(2):
                        ins = pe.matmul(ps[:, 2 * m + t, 0:HALF], a[:, s, k, w], b[:, k, t * HALF:(t + 1) * HALF],
                                        start=(k == 0 and q == 0), stop=(k == KT - 1 and q == 2))
            ins.then_inc(gemm_done, 1)

        def unit(u0, i, s, xh, xl, ready=None):
            pe.wait_ge(w_lo, i * 2 + (u0 + s + 1))
            for m in range(2):
                pe.wait_ge(slot_free[m], i * 2 + tile0(u0 + s) // 2)
                tile(s, m, xh, xl, ready if s == 0 and m == 0 else None)

        def project(u0, units, xh, xl, x0=None, before=lambda i, s: None, after=lambda i, s: None):
            ready = None if x0 is None else (lambda k: pe.wait_ge(xl_ready, x0 + k + 1))
            with pe.Fori(0, units // 2) as i:
                for s in range(2):
                    before(i, s)
                    unit(u0, i, s, xh, xl, ready)
                    after(i, s)

        norm(0)
        project(0, 4, x_h, x_l, X_MIX0)

        def qk_mean(i, s):
            if s == 0:
                pe.wait_ge(slot_free[0], tile0(4) // 2)
            else:
                pe.wait_ge(qk_sq_v, 4)
            pe.wait_ge(qk_norm, i * 2 + (s + 1))
            src = qk_sq[:, bass.ds(i * 2 + s, 1), :].rearrange("p o t -> p (o t)")
            mean_of(sum_ps(s), src, mean_ha).then_inc(qk_ms, 1)

        project(4, 8, x_h, x_l, before=qk_mean)
        pe.wait_ge(wlr_lo, 1)
        pe.wait_ge(qk_std, 8)
        for k in range(KT):
            for q, (a, b) in enumerate(((wlr_h, x_h), (wlr_h, x_l), (wlr_l, x_h))):
                for t in range(2):
                    ins = pe.matmul(ps[:, 4 + t, 0:HALF], a[:, k, :], b[:, k, t * HALF:(t + 1) * HALF],
                                    start=(k == 0 and q == 0), stop=(k == KT - 1 and q == 2))
        ins.then_inc(lr_done, 1)
        pe.wait_ge(slot_free[0], tile0(U_OUT) // 2)
        pe.wait_ge(slot_free[1], tile0(U_OUT) // 2)
        pe.wait_ge(qk_norm, 10)
        for g in range(17):
            if g >= 4:
                pe.wait_ge(rows_out[g % 2], (g - 4) // 2 + 1)
            if g == 15:
                pe.wait_ge(late_landed, 32)
            for n in range(4):
                if g < 15:
                    c = g // 3
                    src = proj[:, (T_K, T_V, T_VB)[g % 3] + n, frames(c)]
                    ins = pe.transpose(ps[0:width(c), g % 4, n * P:(n + 1) * P], src, ident[:])
                else:
                    f = 2 * (g - 15) + n // 2
                    ins = pe.transpose(ps[:, g % 4, n * P:(n + 1) * P], ck_rows[:, n % 2, f * P:(f + 1) * P], ident[:])
            ins.then_inc(rows_T, 1)
        pe.wait_ge(lr_ready, 1)
        for n in range(2):
            mean_of(sum_ps(n), lr, gate_w[:, n * P:(n + 1) * P]).then_inc(gate_done, 1)

        def scores(n):
            h, c = n // 5, n % 5
            b, M = h % 2 * DA, width(c)
            if n >= 2:
                pe.wait_ge(score_read, n - 1)
            q = proj[b:b + DA, T_Q + h // 2, frames(c)]
            k = proj[b:b + DA, T_K + h // 2, :]
            if c < TT:
                ins = pe.matmul(ps[0:M, n % 2, 0:keys(n)], q, k[:, 0:keys(n)], start=True, stop=True)
            else:
                pe.matmul(ps[0:M, n % 2, 0:PAST], q, ck_T[b:b + DA, h // 2, :], start=True, stop=True)
                ins = pe.matmul(ps[0:M, n % 2, PAST:PAST + DEC], q, k[:, SEQ:TOK], start=True, stop=True)
            ins.then_inc(score_done, 1)

        def key_tiles(n):
            return [(j, min(P, keys(n) - j * P)) for j in range((keys(n) + P - 1) // P)]

        def turn(n):
            M = width(n % 5)
            pe.wait_ge(prob_ready, n + 1)
            if n >= 2:
                pe.wait_ge(probT_ready, n - 1)
            for j, w in key_tiles(n):
                ins = pe.transpose(ps[0:w, 2 + n % 2, j * M:(j + 1) * M], prob[0:M, n % 3, j * P:j * P + w],
                                   ident[0:M, 0:M])
            ins.then_inc(probT_done, 1)

        def values(n):
            h, c = n // 5, n % 5
            b, M = h % 2 * DA, width(c)
            pe.wait_ge(probT_ready, n + 1)
            if n >= 2:
                pe.wait_ge(o_copied, n - 1)
            tiles = key_tiles(n)
            for j, w in tiles:
                rows = v_rows[0:w, j, :] if c < TT else (cv_rows[:, j, :] if j < 2 else v_rows[0:w, TT, :])
                ins = pe.matmul(ps[b:b + DA, 4 + n % 2, 0:M], rows[:, h * DA:(h + 1) * DA],
                                prob_T[0:w, n % 2, j * M:(j + 1) * M], start=(j == 0), stop=(j == len(tiles) - 1))
            ins.then_inc(o_done, 1)

        pe.wait_ge(rows_out[0], 9)
        pe.wait_ge(rows_out[1], 8)
        pe.wait_ge(gate_min, 2)
        scores(0)
        scores(1)
        for n in range(5 * HA + 1):
            if n < 5 * HA:
                turn(n)
            if n + 2 < 5 * HA:
                scores(n + 2)
            if n >= 1:
                values(n - 1)

        pe.wait_ge(o_copied, 5 * HA)
        for n in range(2):
            pe.wait_ge(kd_ready, n + 1)
            for c in range(TT + 1):
                M = width(c)
                dst = ps[0:M, kd_bank(n), c * P:(c + 1) * P] if c < TT else ps[0:M, kd_bank(n) + 1, 0:P]
                ins = pe.transpose(dst, kd[:, n, frames(c)], ident[:])
            ins.then_inc(kd_T, 1)

        def head_of(m):
            return 2 * (m // 10) + m % 2, m % 10 // 2, m % 2 * DKB

        def pairs(m):
            h, c, b = head_of(m)
            M = width(c)
            if m % 10 == 0:
                pe.wait_ge(lev_ready, m // 10 + 1)
            if m >= 2:
                pe.wait_ge(masked_done, m - 1)
            for n in range(0 if c < TT else 2, 8):
                l = lev[b:b + DKB, n, frames(c)] if n < 7 else proj[b:b + DKB, T_KB + h // 2, frames(c)]
                r = l if n < 7 else proj[b:b + DKB, T_QB + h // 2, frames(c)]
                at = 2 * (m % 2) + n // 4
                ins = pe.matmul(ps[0:M, at, n % 4 * P:n % 4 * P + M], l, r, start=True, stop=True)
            ins.then_inc(pairs_done, 1)

        def outputs(m):
            h, c, b = head_of(m)
            M = width(c)
            if m >= 2:
                pe.wait_ge(state_ready, m - 1)
            pe.matmul(ps[b:b + DKB, 6 + m % 2, 0:DVB], kd_rows[0:M, c, h * DKB:(h + 1) * DKB],
                      vb_rows[0:M, c, h * DVB:(h + 1) * DVB], start=True, stop=True).then_inc(kv_done, 1)
            pe.wait_ge(pair_ready, m + 1)
            if m >= 2:
                pe.wait_ge(ob_ready, m - 1)
            o = ps[:, 4 + m % 2, 0:M]
            ins = pe.matmul(o, vb_rows[0:M, c, h * DVB:(h + 1) * DVB], pair[0:M, m % 2, 0:M], start=True, stop=(c == 0))
            if c:
                st = state if c < TT else state_s
                ins = pe.matmul(o, st[b:b + DKB, h // 2, :], qe[b:b + DKB, h // 2, frames(c)], start=False, stop=True)
            ins.then_inc(ob_done, 1)

        pe.wait_ge(kd_rows_ready, 2)
        pairs(0)
        for m in range(20):
            if m + 1 < 20:
                pairs(m + 1)
            outputs(m)
        for h in range(HB):
            pe.wait_ge(ob_sq, h + 1)
            if h == 0:
                pe.wait_ge(state_ready, 20)
            if h >= 2:
                pe.wait_ge(ob_std, h - 1)
            mean_of(sum_ps(h % 2), sq[:, h % 2, :], mean_hb).then_inc(ob_ms, 1)

        pe.wait_ge(ob_std, HB)
        project(U_OUT, 4, x_h, x_l, X_CAT)
        norm(1)

        def ffn(layer, u0, x0, last):
            for n, (way, c) in enumerate(FFN_ORDER):
                u = u0 + 4 * n
                if way == "up":
                    project(u, 4, x_h, x_l, x0 if c == 0 else None)
                    continue
                pe.wait_ge(hidl_done, 2 + 32 * layer + 8 * (c + 1))
                if c < NF - 1:
                    project(u, 4, hid_h[c % 2], hid_l[c % 2])
                else:
                    last(u, hid_h[c % 2], hid_l[c % 2])

        ffn(0, U_FFN0, X_FFN0, lambda u, h, l: project(u, 4, h, l))
        norm(2)

        def gated(i, d):
            s = d % 2
            pe.wait_ge(w_lo, i * 2 + (U_PW1 + d + 1))
            for m in range(2):
                pe.wait_ge(slot_free[m], i * 2 + tile0(U_PW1 + d) // 2)
                first = isinstance(i, int) and i + d + m == 0
                tile(s, m, x_h, x_l, (lambda k: pe.wait_ge(xl_ready, X_MIX1 + k + 1)) if first else None)

        def add_taps(i, d):
            m, s = i * 2 + d, d % 2
            pe.wait_ge(diag_ready, m + 1)
            pe.wait_ge(glu_lo, m + 1)
            pe.wait_ge(conv_ready, m + 1)
            for t in range(PE_TAPS):
                for q, (a, b) in enumerate(((diag_h, glu_h), (diag_h, glu_l), (diag_l, glu_h))):
                    for c in range(2):
                        at = t + c * (CW // 2)
                        ins = pe.matmul(sum_ps(1, CW // 2)[:, c, :], a[:, s, t, :], b[:, s, at:at + CW // 2],
                                        start=(t == 0 and q == 0), stop=(t == PE_TAPS - 1 and q == 2))
            ins.then_inc(taps_done, 1)

        def add_mean(i, d, start=False, stop=False):
            pe.wait_ge(conv_ready, i * 2 + (d + 2))
            src = cv[:, bass.ds(i * 2 + d, 1), :].rearrange("p o t -> p (o t)")
            return mean_of(sum_ps(0, CW // 2), src, mean_d, CW // 2, start, stop)

        gated(0, 0)
        gated(0, 1)
        add_taps(0, 0)
        gated(0, 2)
        add_taps(0, 1)
        add_mean(0, 0, start=True)
        with pe.Fori(1, KT // 2 - 1) as i:
            for s in range(2):
                gated(i, s + 1)
                add_taps(i, s)
                add_mean(i, s - 1)
        gated(KT // 2 - 1, 1)
        add_taps(KT // 2 - 1, 0)
        add_mean(KT // 2 - 1, -1)
        for n in range(2):
            pe.wait_ge(slot_free[n], tile0(U_PW2) // 2 - 1)
        for n in range(2):
            at = SEQ if n == 0 else SEQ + PAD + DEC
            for k in range(KT):
                ins = pe.transpose(flat(n)[0:PAD, k * P:(k + 1) * P], glu[:, k, at:at + PAD], ident[:])
            ins.then_inc(gemm_done, 1)
        add_taps(KT // 2 - 1, 1)
        add_mean(KT // 2 - 1, 0)
        add_mean(KT // 2 - 1, 1, stop=True).then_inc(cvmean, 1)
        for k in range(KT):
            pe.wait_ge(cv_sq, k + 1)
            mean_of(sum_ps(1, CW // 2), sq[:, k % 2, :], mean_d, CW // 2, k == 0, k == KT - 1).then_inc(cv_var, 1)
        project(U_PW2, 4, x_h, x_l, X_PW2)
        norm(3)

        def last_down(u, h, l):
            def rows_of(k):
                pe.wait_ge(y_ready, k + 1)
                if k >= 2:
                    pe.wait_ge(y_stage, 2 * (k - 1))
                for c in range(TT + 1):
                    ins = pe.transpose(sum_flat(k % 2)[0:width(c), c * P:(c + 1) * P], y_fin[:, k % 2, frames(c)],
                                       ident[:])
                ins.then_inc(y_T, 1)

            for i in range(2):
                for s in range(2):
                    pe.wait_ge(w_lo, u + 2 * i + s + 1)
                    for m in range(2):
                        k = 4 * i + 2 * s + m
                        pe.wait_ge(slot_free[m], tile0(u + 2 * i + s) // 2)
                        tile(s, m, h, l)
                        if k >= 1:
                            rows_of(k - 1)
            rows_of(KT - 1)

        ffn(1, U_FFN1, X_FFN1, last_down)

    @block.vector
    def _(dve):
        steps = [0]

        def own(ins):
            ins.then_inc(v_step, 1)
            steps[0] += 1
            dve.wait_ge(v_step, steps[0])

        dve.engine_nop().then_inc(hidl_done, 2)
        dve.engine_nop().then_inc(qk_norm, 2)
        dve.engine_nop().then_inc(conv_ready, 1)
        dve.engine_nop().then_inc(taps_done, 2)
        dve.wait_ge(rows_landed, 16 * 19)
        near = 384 + NREL - 1
        dve.tensor_copy(rel_u[:, 0, 0:383], rel[:, NREL - 1:NREL].to_broadcast((HA, 383))).then_inc(rel_built, 1)
        dve.tensor_copy(rel_u[:, 0, 383:near], rel[:, ::-1]).then_inc(rel_built, 1)
        dve.tensor_copy(rel_u[:, 0, near:640], rel[:, 0:1].to_broadcast((HA, 640 - near))).then_inc(rel_built, 1)
        dve.wait_ge(vec_T, 1)
        own(dve.tensor_copy(vecs[:], ps[:, 4, 0:V_N]))
        for k in range(4):
            dve.tensor_scalar(g_qk[:, k:k + 1], vecs[:, V_QG:V_QG + 1], DA ** -0.5, None, ALU.mult)
            dve.tensor_copy(g_qk[:, 4 + k:5 + k], vecs[:, V_KG:V_KG + 1])
        dve.wait_ge(vec_T, 2)
        dve.tensor_copy(w_dw[:].rearrange("p k c -> p (k c)"), ps[:, 5, 0:KT * CONV])
        dve.wait_ge(vec_T, 3)
        dve.tensor_copy(cc_T[:].rearrange("p k c -> p (k c)"), ps[:, 6, 0:KT * PAD]).then_inc(vec_ready, 1)
        dve.wait_ge(wlr_hi, 1)
        dve.tensor_tensor(wlr_l[:, :, 0:RANK], wlr[:], wlr_h[:, :, 0:RANK].bitcast(F32), ALU.subtract)\
            .then_inc(wlr_lo, 1)
        for k in range(KT):
            dve.wait_ge(gemm_done, k + 1)
            dve.tensor_copy(resid[:, k, :], flat(k % 2)[:, 0:TOK]).then_inc(slot_free[k % 2], 1)

        def split_lo(u, i, d):
            s = d % 2
            dve.wait_ge(w_hi, i * 2 + (u + d + 1))
            dve.tensor_tensor(w_l[:, s], w_raw[:, s], w_h[:, s].bitcast(F32), ALU.subtract).then_inc(w_lo, 1)

        def phase(u0, units, evacuate):
            with dve.Fori(0, units // 2) as i:
                for s in range(2):
                    split_lo(u0, i, s + 1)
                    evacuate(i, s)

        def lo(k, x0, src):
            dve.wait_ge(xh_ready, x0 + k + 1)
            dve.tensor_tensor(x_l[:, k, :], src, x_h[:, k, :].bitcast(F32), ALU.subtract).then_inc(xl_ready, 1)

        def norm(n, x0, gain):
            dve.wait_ge(std_ready, n + 1)
            dve.reciprocal(rstd[:, 0:TOK], sumsq[:]).then_inc(rstd_ready, 1)
            dve.wait_ge(rstd_ready, n + 1 + (8 if n else 0))
            for k in range(KT + 1):
                if k < KT:
                    if k >= 3:
                        dve.wait_ge(xl_ready, x0 + k - 2)
                    dve.scalar_tensor_tensor(out=xn[:, k % 3, :], in0=resid[:, k, :],
                                             scalar=vecs[:, gain + k:gain + k + 1], in1=rstd[:, 0:TOK],
                                             op0=ALU.mult, op1=ALU.mult).then_inc(xn_ready, 1)
                if k >= 1:
                    lo(k - 1, x0, xn[:, (k - 1) % 3, :])

        split_lo(0, 0, 0)
        dve.wait_ge(w_dw_hi, 1)
        dve.tensor_tensor(w_dw_l[:], w_dw[:, :, 0:PE_TAPS], w_dw_h[:].bitcast(F32), ALU.subtract)\
            .then_inc(w_dw_lo, 1)
        norm(0, X_MIX0, V_MIX)

        def at(tensor, t):
            return tensor[:, bass.ds(t, 1), :].rearrange("p o t -> p (o t)")

        def evac_qk(i, s):
            dve.wait_ge(gemm_done, i * 4 + (tile0(s) + 2))
            t = i * 4 + (2 * s + 1)
            dve.tensor_copy(halves(at(proj, t)), slot(1)).then_inc(slot_free[1], 1)
            dve.wait_ge(slot_free[1], i * 2 + (tile0(s) // 2 + 1))
            dve.tensor_tensor(at(qk_sq, t), at(proj, t), at(proj, t), ALU.mult).then_inc(qk_sq_v, 1)

        def evac_rest(i, s):
            dve.wait_ge(gemm_done, i * 4 + (tile0(4 + s) + 2))
            dve.tensor_copy(halves(at(proj, i * 4 + (8 + 2 * s + 1))), slot(1)).then_inc(slot_free[1], 1)
            t = i * 2 + s
            dve.wait_ge(qk_std, t + 1)
            dve.reciprocal(rstd[:, 0:TOK], sumsq[:]).then_inc(rstd_ready, 1)
            dve.wait_ge(rstd_ready, t + 2)
            dve.scalar_tensor_tensor(out=at(proj, t), in0=at(proj, t), scalar=g_qk[:, bass.ds(t, 1)],
                                     in1=rstd[:, 0:TOK], op0=ALU.mult, op1=ALU.mult).then_inc(qk_norm, 1)

        phase(0, 4, evac_qk)
        phase(4, 8, evac_rest)

        for g in range(1, 17, 2):
            dve.wait_ge(rows_T, g + 1)
            dst, src = rows_group(g)
            dve.tensor_copy(dst, src).then_inc(rows_out[1], 1)

        dve.wait_ge(rows_T, 15)
        for n in range(2):
            dve.wait_ge(gate_abs, n + 1)
            own(dve.tensor_scalar(halves(gl_b[:]), sum_ps(n), vecs[:, V_GB + n:V_GB + n + 1], 0.0, ALU.add, ALU.min))
            dve.wait_ge(gate_ln, 2 * n + 1)
            dve.tensor_tensor(gl_b[:], gl_b[:], gl_a[:], ALU.subtract).then_inc(gate_ln, 1)
            dve.wait_ge(gate_ln, 2 * n + 2)
            for c in range(TT + 1):
                dve.tensor_tensor_scan(bt[:, n, frames(c)], ones[:, 0:width(c)], gl_b[:, frames(c)], 0.0,
                                       ALU.mult, ALU.add).then_inc(bt_ready, 1)
            dve.wait_ge(bt_ready, 5 * (n + 1))
            dve.engine_nop().then_inc(gate_min, 1)

        def biased(n):
            h, c = n // 5, n % 5
            M, nk = width(c), keys(n)
            first = 512 - nk if c < TT else 384 - PAST
            dve.wait_ge(score_done, n + 1)
            if c == 0:
                dve.wait_ge(bias_ready, h + 1)
            if n >= 3:
                dve.wait_ge(probT_done, n - 2)
            dve.tensor_tensor_reduce(prob[0:M, n % 3, 0:nk], ps[0:M, n % 2, 0:nk], bias[0:M, h % 2, first:first + nk],
                                     1.0, -3.0e38, ALU.add, ALU.max, small[0:M, n % 3:n % 3 + 1])\
                .then_inc(score_read, 1)
            dve.wait_ge(score_read, n + 1)
            dve.tensor_scalar(small[0:M, 4 + n % 3:5 + n % 3], small[0:M, n % 3:n % 3 + 1], -1.0, None, ALU.mult)\
                .then_inc(nmax_ready, 1)

        def normalised(n):
            M, nk = width(n % 5), keys(n)
            dve.wait_ge(exp_done, n + 1)
            own(dve.reciprocal(small[0:M, 12 + n % 3:13 + n % 3], small[0:M, 8 + n % 3:9 + n % 3]))
            dve.tensor_scalar(prob[0:M, n % 3, 0:nk], prob[0:M, n % 3, 0:nk], small[0:M, 12 + n % 3:13 + n % 3], None,
                              ALU.mult).then_inc(prob_ready, 1)

        for n in range(5 * HA + 1):
            if n < 5 * HA:
                biased(n)
            if n >= 1:
                normalised(n - 1)

        dve.wait_ge(o_copied, 5 * HA)
        dve.wait_ge(stored, 16 * 4)
        for n in range(2):
            for seg, w in ((slice(0, SEQ), P), (slice(SEQ, TOK), DEC)):
                b = bt[:, n, seg].rearrange("p (c t) -> p c t", t=w)
                ins = dve.tensor_tensor(kd[:, n, seg].rearrange("p (c t) -> p c t", t=w),
                                        b[:, :, w - 1:w].to_broadcast((P, (seg.stop - seg.start) // w, w)), b,
                                        ALU.subtract)
            ins.then_inc(kd_diff, 1)
        for n in range(2):
            dve.wait_ge(kd_exp, n + 1)
            dve.tensor_tensor(kd[:, n, :], kd[:, n, :], proj[:, T_KB + n, :], ALU.mult).then_inc(kd_ready, 1)
            dve.wait_ge(eb_ready, n + 1)
            dve.scalar_tensor_tensor(out=qe[:, n, :], in0=proj[:, T_QB + n, :], scalar=DKB ** -0.5, in1=eb[:, n, :],
                                     op0=ALU.mult, op1=ALU.mult).then_inc(kd_ready, 1) if n == 1 else \
                own(dve.scalar_tensor_tensor(out=qe[:, n, :], in0=proj[:, T_QB + n, :], scalar=DKB ** -0.5,
                                             in1=eb[:, n, :], op0=ALU.mult, op1=ALU.mult))

        def by_level(n):
            for l, s in enumerate(levels()):
                cols = slice(0, SEQ if s > 16 else TOK)
                split = lambda t: t[:, cols].rearrange("p (a h c) -> p a h c", h=2, c=s)
                yield s, split(lev[:, l, :]), split(bt[:, n, :]), split(proj[:, T_KB + n, :]), \
                    split(proj[:, T_QB + n, :])

        def mask_pairs(m):
            c = m % 10 // 2
            M, l0 = width(c), (0 if c < TT else 2)
            dve.wait_ge(pairs_done, m + 1)
            src = ps[0:M, 2 * (m % 2):2 * (m % 2) + 2, :].rearrange("p a (l i) -> p (a l) i", i=P)[:, l0:8, 0:M]
            own(dve.tensor_tensor(masked[0:M, m % 2, l0:8, 0:M], src, masks[0:M, l0:8, 0:M], ALU.mult))
            if m >= 2:
                dve.wait_ge(ob_done, m - 1)
            dve.engine_nop().then_inc(masked_done, 1)
            dve.tensor_reduce(pair[0:M, m % 2, 0:M], masked[0:M, m % 2, l0:8, 0:M].rearrange("p l i -> p i l"), AX.X,
                              ALU.add).then_inc(pair_ready, 1)

        def new_state(m):
            h, c, b = 2 * (m // 10) + m % 2, m % 10 // 2, m % 2 * DKB
            dve.wait_ge(kv_done, m + 1)
            dve.wait_ge(ob_done, m + 1)
            kv = ps[b:b + DKB, 6 + m % 2, 0:DVB]
            st = (state if c < TT else state_s)[b:b + DKB, h // 2, :]
            if c == 0:
                dve.tensor_copy(st, kv).then_inc(state_ready, 1)
            else:
                last = frames(c).stop - 1
                dve.scalar_tensor_tensor(out=st, in0=st, scalar=eb[b:b + DKB, h // 2, last:last + 1], in1=kv,
                                         op0=ALU.mult, op1=ALU.add).then_inc(state_ready, 1)

        for n in range(2):
            if n:
                dve.wait_ge(pairs_done, 10)
            for s, z, b, k, q in by_level(n):
                na = z.shape[1]
                ref = b[:, :, 0, s - 1:s].to_broadcast((P, na, s))
                dve.tensor_tensor(z[:, :, 0, :], ref, b[:, :, 0, :], ALU.subtract)
                ins = dve.tensor_tensor(z[:, :, 1, :], b[:, :, 1, :], ref, ALU.subtract)
            ins.then_inc(lev_diff, 1)
            dve.wait_ge(lev_exp, n + 1)
            for s, z, b, k, q in by_level(n):
                dve.tensor_tensor(z[:, :, 0, :], z[:, :, 0, :], k[:, :, 0, :], ALU.mult)
                ins = dve.tensor_tensor(z[:, :, 1, :], z[:, :, 1, :], q[:, :, 1, :], ALU.mult)
            ins.then_inc(lev_ready, 1)
            for m in range(10 * n, 10 * n + 10):
                mask_pairs(m)
                if m >= 1:
                    new_state(m - 1)
        new_state(19)
        dve.wait_ge(silu_done, 1)
        for h in range(HB):
            dve.wait_ge(ob_std, h + 1)
            own(dve.reciprocal(rstd[:, 0:TOK], sumsq[:]))
            o = proj[:, T_VB + h, :]
            own(dve.scalar_tensor_tensor(out=o, in0=o, scalar=vecs[:, V_ON:V_ON + 1], in1=rstd[:, 0:TOK],
                                         op0=ALU.mult, op1=ALU.mult))
            dve.tensor_tensor(o, o, proj[:, T_GB + h, :], ALU.mult).then_inc(ob_cat, 1)
        for k in range(KT):
            lo(k, X_CAT, proj[:, T_Q + k if k < 4 else T_VB + k - 4, :])

        def add_resid(u0, bias_at=None):
            def evacuate(i, s):
                for m in range(2):
                    k = i * 4 + (2 * s + m)
                    dve.wait_ge(gemm_done, i * 4 + (tile0(u0 + s) + m + 1))
                    r = halves(at(resid, k))
                    if bias_at is None:
                        dve.tensor_tensor(r, slot(m), r, ALU.add).then_inc(slot_free[m], 1)
                    else:
                        dve.scalar_tensor_tensor(out=r, in0=slot(m), scalar=vecs[:, bass.ds(k + bias_at, 1)], in1=r,
                                                 op0=ALU.add, op1=ALU.add).then_inc(slot_free[m], 1)
            return evacuate

        def hidden(layer, c, u0):
            base = 32 * layer + 8 * c

            def evacuate(i, s):
                for m in range(2):
                    t = i * 4 + (2 * s + m)
                    dve.wait_ge(slot_free[m], i * 2 + (tile0(u0 + s) // 2 + 1))
                    dve.wait_ge(hidl_done, t + base + 1)
                    dve.tensor_tensor(relu2[:, m, :], relu[:, m, :], relu[:, m, :], ALU.mult).then_inc(relu2_done, 1)
                    dve.wait_ge(hidh_done, t + (base + 1))
                    dve.tensor_tensor(at(hid_l[c % 2], t), relu2[:, m, :], at(hid_h[c % 2], t).bitcast(F32),
                                      ALU.subtract).then_inc(hidl_done, 1)
            return evacuate

        def ffn(layer, u0, last):
            for n, (way, c) in enumerate(FFN_ORDER):
                u = u0 + 4 * n
                if way == "up":
                    phase(u, 4, hidden(layer, c, u))
                elif c < NF - 1:
                    phase(u, 4, add_resid(u))
                else:
                    last(u)

        phase(U_OUT, 4, add_resid(U_OUT))
        norm(1, X_FFN0, V_FFN)
        ffn(0, U_FFN0, lambda u: phase(u, 4, add_resid(u)))
        norm(2, X_MIX1, V_MIX + 8)

        dve.wait_ge(glu_edges, 3)

        def glu_conv(i, s):
            m = i * 2 + s
            dve.wait_ge(slot_free[0], m + (tile0(U_PW1) // 2 + 1))
            dve.wait_ge(gemm_done, i * 4 + (tile0(U_PW1 + s) + 2))
            u = at(glu, m)
            for to, ps_part, frames_ in ((PAD, ps[:, 2, 0:HALF], slice(0, HALF)),
                                         (PAD + HALF, ps[:, 3, 0:SEQ - HALF], slice(HALF, SEQ)),
                                         (2 * PAD + SEQ, ps[:, 3, SEQ - HALF:HALF], slice(SEQ, TOK))):
                n = frames_.stop - frames_.start
                ins = dve.scalar_tensor_tensor(out=u[:, to:to + n], in0=ps_part,
                                               scalar=vecs[:, bass.ds(m + V_B1, 1)], in1=sig[:, s, frames_],
                                               op0=ALU.add, op1=ALU.mult)
            ins.then_inc(slot_free[1], 1)
            dve.wait_ge(slot_free[1], m + (tile0(U_PW1) // 2 + 1))
            y, odd = at(cv, m), rstd[:]
            w = w_dw[:].rearrange("p k c -> p (k c)")
            taps = range(PE_TAPS, CONV)
            for n, t in enumerate(taps):
                to = (y, odd)[n % 2]
                tap = w[:, bass.ds(m * CONV + t, 1)]
                src = u[:, t:t + CW]
                if n == 0:
                    ins = dve.tensor_scalar(y, src, tap, vecs[:, bass.ds(m + V_BDW, 1)], ALU.mult, ALU.add)
                elif n == 1:
                    dve.wait_ge(conv_ready, m + 1)
                    ins = dve.tensor_scalar(odd, src, tap, None, ALU.mult)
                    ins.then_inc(conv_step, 1)
                    dve.wait_ge(glu_hi, m + 1)
                    dve.tensor_tensor(glu_l[:, s, :], u, glu_h[:, s, :].bitcast(F32), ALU.subtract)\
                        .then_inc(glu_lo, 1)
                    continue
                else:
                    dve.wait_ge(conv_step, m * (len(taps) + 1) + (n - 1))
                    ins = dve.scalar_tensor_tensor(out=to, in0=src, scalar=tap, in1=to, op0=ALU.mult, op1=ALU.add)
                ins.then_inc(conv_step, 1)
            dve.wait_ge(taps_done, m + 3)
            dve.wait_ge(conv_step, m * (len(taps) + 1) + len(taps))
            yh = y.rearrange("p (a t) -> p a t", a=2)
            dve.tensor_tensor(yh, sum_ps(1, CW // 2), yh, ALU.add).then_inc(conv_step, 1)
            dve.wait_ge(conv_step, m * (len(taps) + 1) + (len(taps) + 1))
            dve.tensor_tensor(y, y, odd, ALU.add).then_inc(conv_ready, 1)

        phase(U_PW1, 8, glu_conv)
        dve.wait_ge(gemm_done, tile0(U_PW2))
        dve.tensor_copy(ccn[:, 1, :], flat(1)[0:PAD, :]).then_inc(slot_free[1], 1)
        dve.wait_ge(cvmean, 1)
        for k in range(KT):
            y = cv[:, k, :].rearrange("p (a t) -> p a t", a=2)
            dve.scalar_tensor_tensor(out=y, in0=sum_ps(0, CW // 2), scalar=-1.0, in1=y, op0=ALU.mult, op1=ALU.add)\
                .then_inc(cv_centred, 1)
        dve.wait_ge(cv_std, 1)
        own(dve.reciprocal(rstd[:], rstd[:]))
        for k in range(KT + 1):
            if k < KT:
                dve.tensor_tensor(cv[:, k, :], cv[:, k, :], rstd[:], ALU.mult).then_inc(cv_norm, 1)
            if k >= 1:
                lo(k - 1, X_PW2, xn[:, (k - 1) % 3, :])
        phase(U_PW2, 4, add_resid(U_PW2, V_B2))
        norm(3, X_FFN1, V_FFN + 8)
        dve.wait_ge(stored, 16 * 8)

        def y_out(u):
            for i in range(2):
                for s in range(2):
                    if u + 2 * i + s + 1 < U_END:
                        split_lo(u, i, s + 1)
                    for m in range(2):
                        k = 4 * i + 2 * s + m
                        dve.wait_ge(gemm_done, tile0(u + 2 * i + s) + m + 1)
                        if k >= 2:
                            dve.wait_ge(y_T, k - 1)
                        dve.tensor_tensor(halves(y_fin[:, k % 2, :]), slot(m), halves(resid[:, k, :]), ALU.add)\
                            .then_inc(y_ready, 1)
                        dve.wait_ge(y_ready, k + 1)
                        dve.engine_nop().then_inc(slot_free[m], 1)

        ffn(1, U_FFN1, y_out)

    ctx.close()


_INS = ["x_prompt", "x_sample", "cache_a_k", "cache_a_v", "state_b", "cache_c", "norm_mix_g", "norm_ffn_g",
        "w_in_ab", "a_q_norm_g", "a_k_norm_g", "a_rel_bias", "b_gate_w_up", "b_gate_b", "b_out_norm_g", "w_out_ab",
        "c_w_pw1", "c_b_pw1", "c_w_dw", "c_b_dw", "c_ln_g", "c_ln_b", "c_w_pw2", "c_b_pw2", "w_ffn_up",
        "w_ffn_down"]
_OUTS = [("y_prompt", (1, 512, 1024)), ("y_sample", (1, 32, 1024)),
         ("ak_prompt", (1, 1, 512, 8, 64)), ("av_prompt", (1, 1, 512, 8, 64)),
         ("ak_sample", (1, 1, 32, 8, 64)), ("av_sample", (1, 1, 32, 8, 64)),
         ("sb_prompt", (1, 1, 4, 64, 128)), ("sb_sample", (1, 1, 4, 64, 128)),
         ("cc_prompt", (1, 1, 30, 1024)), ("cc_sample", (1, 1, 30, 1024))]


def kernel(**inputs):
    import numpy as np
    from concourse import bacc
    from concourse.bass_utils import run_bass_kernel_spmd

    nc = bacc.Bacc("TRN2", target_bir_lowering=False, num_devices=1)
    arrays, args = {}, {}
    for name in _INS:
        a = np.asarray(inputs[name])
        if name == "c_w_pw1":
            a = a.reshape(1, D, 2, KT, P)[:, :, ::-1].transpose(0, 1, 3, 2, 4).reshape(1, D, 2 * D)
        a = np.ascontiguousarray(a)
        arrays[f"in_{name}"] = a
        args[name] = nc.dram_tensor(f"in_{name}", a.shape, mybir.dt.from_np(a.dtype), kind="ExternalInput").ap()
    for name, shape in _OUTS:
        args[name] = nc.dram_tensor(f"out_{name}", shape, F32, kind="ExternalOutput").ap()
    hybrid_kernel(nc, **args)
    r = run_bass_kernel_spmd(nc, [arrays], core_ids=[0])
    return tuple(r.results[0][f"out_{name}"] for name, _ in _OUTS)
```

```python
from contextlib import ExitStack

import concourse.bass as bass
from concourse import mybir

F32 = mybir.dt.float32
F32R = mybir.dt.float32r
ACT = mybir.ActivationFunctionType
ALU = mybir.AluOpType
AX = mybir.AxisListType

P = 128
D = 1024
KT = D // P
SEQ, DEC = 512, 32
TOK = SEQ + DEC
HALF = TOK // 2
TT = SEQ // P
NF = 4 * D // D
CHUNK = 64
HA, DA = 8, 64
HB, DKB, DVB = 4, 64, 128
PAST = 256
NREL = 192
RANK = 16
CONV = 31
PAD = CONV - 1
CW = SEQ + PAD + DEC + 2
PE_TAPS = 11
FW = PAD + CW
EPS = 1e-6
NEG = -1e30

U_IN, U_OUT, U_FFN0 = 0, 12, 16
U_PW1 = U_FFN0 + 8 * NF
U_PW2 = U_PW1 + 8
U_FFN1 = U_PW2 + 4
U_END = U_FFN1 + 8 * NF
FFN_ORDER = [("up", 0)] + [s for c in range(1, NF) for s in (("up", c), ("down", c - 1))] + [("down", NF - 1)]

X_MIX0, X_CAT, X_FFN0, X_MIX1, X_PW2, X_FFN1 = (8 * n for n in range(6))

V_MIX, V_FFN, V_B1, V_BDW, V_LNG, V_LNB, V_B2, V_GB, V_ON, V_QG, V_KG = 0, 16, 32, 48, 56, 64, 72, 80, 82, 83, 84
V_N = 85

T_Q, T_K, T_V, T_QB, T_KB, T_VB, T_GB = 0, 4, 8, 12, 14, 16, 20
N_PROJ = 24


def tile0(u):
    return 8 + 2 * u + (2 if u >= U_PW2 else 0)


def levels():
    return [64 >> n for n in range(7)]


def hybrid_kernel(nc, x_prompt, x_sample, cache_a_k, cache_a_v, state_b, cache_c, norm_mix_g, norm_ffn_g,
                  w_in_ab, a_q_norm_g, a_k_norm_g, a_rel_bias, b_gate_w_up, b_gate_b, b_out_norm_g, w_out_ab,
                  c_w_pw1, c_b_pw1, c_w_dw, c_b_dw, c_ln_g, c_ln_b, c_w_pw2, c_b_pw2, w_ffn_up, w_ffn_down,
                  y_prompt, y_sample, ak_prompt, av_prompt, ak_sample, av_sample, sb_prompt, sb_sample,
                  cc_prompt, cc_sample):
    ctx = ExitStack()

    def sb(stack, name, shape, dt=F32):
        return stack.enter_context(nc.sbuf_tensor(name, shape, dt))

    def sem(name):
        return ctx.enter_context(nc.semaphore(name))

    resid = sb(ctx, "resid", [P, KT, TOK])
    w_raw = sb(ctx, "w_raw", [P, 2, KT, 256])
    with ExitStack() as over:
        w_h = sb(over, "w_h", [P, 2, KT, 256], F32R)
        w_l = sb(over, "w_l", [P, 2, KT, 256], F32R)
    lev = sb(ctx, "lev", [P, 7, 2, TOK])
    sb(ctx, "under_w", [P, 4 * KT * 256 - 14 * TOK])
    ident = sb(ctx, "ident", [P, P])
    ones = sb(ctx, "ones", [P, P])
    mean_d = sb(ctx, "mean_d", [P, P])
    mean_ha = sb(ctx, "mean_ha", [P, P])
    mean_hb = sb(ctx, "mean_hb", [P, P])
    masks = sb(ctx, "masks", [P, 8, P])
    vec_rows = sb(ctx, "vec_rows", [V_N, P])
    vecs = sb(ctx, "vecs", [P, V_N])
    g_qk = sb(ctx, "g_qk", [P, 8])
    eps = sb(ctx, "eps", [P, 1])
    w_dw = sb(ctx, "w_dw", [P, KT, CONV])
    w_dw_h = sb(ctx, "w_dw_h", [P, KT, PE_TAPS], F32R)
    w_dw_l = sb(ctx, "w_dw_l", [P, KT, PE_TAPS])
    cc_T = sb(ctx, "cc_T", [P, KT, PAD])
    gate_w = sb(ctx, "gate_w", [RANK, HB * DKB])
    state = sb(ctx, "state", [P, 2, DVB])
    state_s = sb(ctx, "state_s", [P, 2, DVB])
    sq = sb(ctx, "sq", [P, 2, CW])
    sumsq = sb(ctx, "sumsq", [P, TOK])
    rstd = sb(ctx, "rstd", [P, CW])
    xn = sb(ctx, "xn", [P, 3, TOK])
    small = sb(ctx, "small", [P, 16])

    with ExitStack() as over:
        x_h = sb(over, "x_h", [P, KT, TOK], F32R)
        x_l = sb(over, "x_l", [P, KT, TOK], F32R)
        xf_h = sb(over, "xf_h", [P, KT, TOK], F32R)
        odd_h = sb(over, "odd_h", [P, KT, TOK], F32R)
        xf_l = sb(over, "xf_l", [P, KT, TOK], F32R)
        odd_l = sb(over, "odd_l", [P, KT, TOK], F32R)
        hid_h, hid_l = (x_h, odd_h), (x_l, odd_l)
        relu = sb(over, "relu", [P, 2, TOK])
        relu2 = sb(over, "relu2", [P, 2, TOK])
    with ExitStack() as over:
        v_rows = sb(over, "v_rows", [P, TT + 1, HA * DA])
        vb_rows = sb(over, "vb_rows", [P, TT + 1, HB * DVB])
        with ExitStack() as att:
            k_rows = sb(att, "k_rows", [P, TT + 1, HA * DA])
            ck_T = sb(att, "ck_T", [P, 4, PAST])
        kd = sb(over, "kd", [P, 2, TOK])
        qe = sb(over, "qe", [P, 2, TOK])
        kd_rows = sb(over, "kd_rows", [P, TT + 1, HB * DKB])
    with ExitStack() as over:
        masked = sb(over, "masked", [P, 2, 8, P])
        pair = sb(over, "pair", [P, 2, P])
    with ExitStack() as over:
        sb(over, "under_x", [P, 2, KT, TOK])
        with ExitStack() as mix:
            x_rows = sb(mix, "x_rows", [P, TT + 1, D])
            dw_rows = sb(mix, "dw_rows", [CONV, D])
            cc_rows = sb(mix, "cc_rows", [PAD, D])
        with ExitStack() as mix:
            proj = sb(mix, "proj", [P, N_PROJ, TOK])
            lr = sb(mix, "lr", [RANK, TOK])
            with ExitStack() as part:
                qk_sq = sb(part, "qk_sq", [P, 8, TOK])
                wlr = sb(part, "wlr", [P, KT, RANK])
                wlr_h = sb(part, "wlr_h", [P, KT, P], F32R)
                wlr_l = sb(part, "wlr_l", [P, KT, P], F32R)
            with ExitStack() as part:
                ck_rows = sb(part, "ck_rows", [P, 2, HA * DA])
                cv_rows = sb(part, "cv_rows", [P, 2, HA * DA])
                bias = sb(part, "bias", [P, 2, 512])
                prob = sb(part, "prob", [P, 4, 512])
                prob_T = sb(part, "prob_T", [P, 2, 512])
            rel = sb(mix, "rel", [HA, NREL])
            rel_u = sb(mix, "rel_u", [HA, 1, 640])
        with ExitStack() as mix:
            glu = sb(mix, "glu", [P, KT, FW])
            cv = sb(mix, "cv", [P, KT, CW])
            sig = sb(mix, "sig", [P, 2, TOK])
            glu_h = sb(mix, "glu_h", [P, 2, FW], F32R)
            glu_l = sb(mix, "glu_l", [P, 2, FW], F32R)
            with ExitStack() as part:
                diag_h = sb(part, "diag_h", [P, 2, PE_TAPS, P], F32R)
                diag_l = sb(part, "diag_l", [P, 2, PE_TAPS, P], F32R)
            ccn = sb(mix, "ccn", [PAD, 2, D])
        y_rows = sb(over, "y_rows", [P, 2, TT + 1, P])
        y_fin = sb(over, "y_fin", [P, 2, TOK])
    r_tok = xn[:, 0, :]
    gl_a, gl_b = xn[:, 1, :], xn[:, 2, :]
    bt = proj[:, T_V:T_V + 2, :]
    eb = proj[:, T_V + 2:T_V + 4, :]
    ps = ctx.enter_context(nc.psum_tensor("ps", [P, 8, 512], F32))
    rel_dram = nc.dram_tensor("rel_scratch", (HA, P, 640), F32, kind="Internal").ap()

    def slot(m):
        return ps[:, 2 * m:2 * m + 2, 0:HALF]

    def flat(m):
        return ps[:, 2 * m:2 * m + 2, :].rearrange("p a b -> p (a b)")

    def halves(ap):
        return ap.rearrange("p (a t) -> p a t", a=2)

    def sum_ps(n, w=HALF):
        return ps[:, 4 + 2 * n:6 + 2 * n, 0:w]

    def frames(c):
        return slice(c * P, c * P + (P if c < TT else DEC))

    def width(c):
        return P if c < TT else DEC

    x_landed = [sem(f"x_landed{c}") for c in range(TT + 1)]
    gains_landed, rows_landed = sem("gains_landed"), sem("rows_landed")
    late_landed = sem("late_landed")
    w_landed = [sem("w_landed0"), sem("w_landed1")]
    w_hi, w_lo = sem("w_hi"), sem("w_lo")
    consts = sem("consts")
    gains_T, gains_ready = sem("gains_T"), sem("gains_ready")
    r_ready = sem("r_ready")
    vec_T = sem("vec_T")
    vec_ready = sem("vec_ready")
    gemm_done = sem("gemm_done")
    slot_free = [sem("slot_free0"), sem("slot_free1")]
    sq_ready, sumsq_step, ms_ready, std_ready, rstd_ready = (sem(n) for n in (
        "sq_ready", "sumsq_step", "ms_ready", "std_ready", "rstd_ready"))
    xn_ready, xh_ready, xl_ready = sem("xn_ready"), sem("xh_ready"), sem("xl_ready")
    relu2_done, hidh_done, hidl_done = sem("relu2_done"), sem("hidh_done"), sem("hidl_done")
    wlr_hi, wlr_lo = sem("wlr_hi"), sem("wlr_lo")
    qk_sq_ready, qk_ms, qk_std, qk_norm = (sem(n) for n in ("qk_sq_ready", "qk_ms", "qk_std", "qk_norm"))
    rel_built, rel_stored, bias_landed, bias_ready = (sem(n) for n in (
        "rel_built", "rel_stored", "bias_landed", "bias_ready"))
    lr_done, lr_ready, gate_done, gate_abs, gate_min, gate_ln, bt_ready, eb_ready = (sem(n) for n in (
        "lr_done", "lr_ready", "gate_done", "gate_abs", "gate_min", "gate_ln", "bt_ready", "eb_ready"))
    rows_T = sem("rows_T")
    rows_out = [sem("rows_out_a"), sem("rows_out_v")]
    silu_done = sem("silu_done")
    score_done, score_read, nmax_ready, exp_done, prob_ready, probT_done, probT_ready, o_done, o_copied = (
        sem(n) for n in ("score_done", "score_read", "nmax_ready", "exp_done", "prob_ready", "probT_done",
                         "probT_ready", "o_done", "o_copied"))
    lev_diff, lev_exp, lev_ready, kd_diff, kd_exp, kd_ready, kd_T, kd_rows_ready = (sem(n) for n in (
        "lev_diff", "lev_exp", "lev_ready", "kd_diff", "kd_exp", "kd_ready", "kd_T", "kd_rows_ready"))
    pairs_done, masked_done, pair_ready, kv_done, state_ready, ob_done, ob_ready = (sem(n) for n in (
        "pairs_done", "masked_done", "pair_ready", "kv_done", "state_ready", "ob_done", "ob_ready"))
    ob_sq, ob_ms, ob_std, ob_cat = (sem(n) for n in ("ob_sq", "ob_ms", "ob_std", "ob_cat"))
    w_dw_hi, w_dw_lo, glu_hi, glu_lo, diag_ready, taps_done = (
        sem(n) for n in ("w_dw_hi", "w_dw_lo", "glu_hi", "glu_lo", "diag_ready", "taps_done"))
    glu_edges, conv_step, conv_ready, cvmean, cv_centred, cv_sq, cv_var, cv_std, cv_norm, cv_silu = (
        sem(n) for n in ("glu_edges", "conv_step", "conv_ready", "cvmean", "cv_centred", "cv_sq",
                         "cv_var", "cv_std", "cv_norm", "cv_silu"))
    y_ready, y_T, y_stage = sem("y_ready"), sem("y_T"), sem("y_stage")
    y_stored = [sem("y_stored0"), sem("y_stored1")]
    a_step, v_step, p_step = sem("a_step"), sem("v_step"), sem("p_step")
    stored = sem("stored")

    def sum_flat(n):
        return ps[:, 4 + 2 * n:6 + 2 * n, :].rearrange("p a b -> p (a b)")

    def keys(n):
        return (n % 5 + 1) * P if n % 5 < TT else PAST + DEC

    def kd_bank(n):
        return 6 - 2 * n

    def rows_group(g):
        if g < 15:
            c, kind = g // 3, g % 3
            M = width(c)
            return (k_rows, v_rows, vb_rows)[kind][0:M, c, :], ps[0:M, g % 4, :]
        q = g - 15
        return ck_T[:, 2 * q:2 * q + 2, :].rearrange("p a t -> p (a t)"), ps[:, g % 4, :]

    def ob_root(act, h):
        act.wait_ge(ob_ms, h + 1)
        if h >= 1:
            act.wait_ge(ob_cat, h)
        act.activation(halves(sumsq[:]), sum_ps(h % 2), ACT.Sqrt, bias=eps[:, 0:1]).then_inc(ob_std, 1)

    block = ctx.enter_context(nc.Block())

    def w_view(w):
        return w.rearrange("(k p) n -> p k n", p=P)

    @block.sync
    def _(sp):
        xp = x_prompt[0].rearrange("(c p) d -> c p d", p=P)
        for c in range(TT):
            sp.dma_start(x_rows[:, c, :], xp[c]).then_inc(x_landed[c], 16)
        sp.dma_start(x_rows[0:DEC, TT, :], x_sample[0]).then_inc(x_landed[TT], 16)

        def stream(u0, units, source, first=False):
            if first:
                for s in range(2):
                    sp.dma_start(w_raw[:, s], source(s)).then_inc(w_landed[s], 16)
            with sp.Fori(1 if first else 0, units // 2) as i:
                for s in range(2):
                    sp.wait_ge(w_lo, i * 2 + (u0 + s - 1))
                    sp.dma_start(w_raw[:, s], source(i * 2 + s)).then_inc(w_landed[s], 16)

        def columns(w, at=0):
            v = w_view(w)
            return lambda n: v[:, :, bass.ds(n * 256 + at, 256)]

        def ffn(layer, u0):
            for n, (way, c) in enumerate(FFN_ORDER):
                src = (columns(w_ffn_up[layer], c * D) if way == "up"
                       else columns(w_ffn_down[layer][c * D:(c + 1) * D, :]))
                stream(u0 + 4 * n, 4, src)

        stream(U_IN, 12, columns(w_in_ab[0]), first=True)
        stream(U_OUT, 4, columns(w_out_ab[0]))
        ffn(0, U_FFN0)
        stream(U_PW1, 8, columns(c_w_pw1[0]))
        stream(U_PW2, 4, columns(c_w_pw2[0]))
        ffn(1, U_FFN1)
        yp = y_prompt[0].rearrange("(c p) d -> p c d", p=P)
        for k in range(KT):
            sp.wait_ge(y_stage, 2 * (k + 1))
            sp.dma_start(yp[:, :, k * P:(k + 1) * P], y_rows[:, k % 2, 0:TT, :]).then_inc(y_stored[k % 2], 16)
            sp.dma_start(y_sample[0][:, k * P:(k + 1) * P], y_rows[0:DEC, k % 2, TT, :])\
                .then_inc(y_stored[k % 2], 16)
        for n in range(2):
            sp.wait_ge(y_stored[n], 32 * (KT // 2))

    @block.gpsimd
    def _(pool):
        steps = [0]

        def own(ins):
            ins.then_inc(p_step, 1)
            steps[0] += 1
            pool.wait_ge(p_step, steps[0])

        pool.memset(ones[:], 1.0)
        pool.memset(mean_d[:], 1.0 / D)
        pool.memset(mean_hb[:], 1.0 / DVB)
        pool.memset(eps[:], EPS)
        pool.memset(wlr_h[:].bitcast(F32), 0.0)
        pool.memset(wlr_l[:].bitcast(F32), 0.0)
        pool.memset(mean_ha[:], 0.0)
        own(pool.memset(ident[:], 0.0))
        own(pool.affine_select(out=ident[:], in_=ident[:], compare_op=ALU.not_equal, fill=1.0, base=0,
                               pattern=[[-1, P]], channel_multiplier=1))
        own(pool.memset(mean_ha[0:DA, 0:DA], 1.0 / DA))
        pool.memset(mean_ha[DA:P, DA:P], 1.0 / DA).then_inc(consts, 1)
        pool.wait_ge(consts, 1)
        own(pool.memset(masks[:], 0.0))
        for n, s in enumerate(levels()):
            second = masks[:, n, :].rearrange("p (a h c) -> p a h c", h=2, c=s)[:, :, 1, :]
            na = P // (2 * s)
            own(pool.memset(second, DKB ** -0.5))
            own(pool.affine_select(out=second, in_=second, compare_op=ALU.is_ge, fill=0.0, base=0,
                                   pattern=[[-2 * s, na], [0, s]], channel_multiplier=1))
            own(pool.affine_select(out=second, in_=second, compare_op=ALU.is_ge, fill=0.0, base=s - 1,
                                   pattern=[[2 * s, na], [0, s]], channel_multiplier=-1))
        pool.affine_select(out=masks[:, 7, :], in_=masks[:, 7, :], compare_op=ALU.not_equal, fill=DKB ** -0.5,
                           base=0, pattern=[[-1, P]], channel_multiplier=1).then_inc(consts, 1)

        def sum_squares(n, k, parity, first):
            pool.wait_ge(sq_ready, k + (8 * n + 1))
            if first:
                pool.tensor_copy(sumsq[:], sq[:, parity, 0:TOK]).then_inc(sumsq_step, 1)
            else:
                pool.wait_ge(sumsq_step, k + 8 * n)
                pool.tensor_tensor(sumsq[:], sumsq[:], sq[:, parity, 0:TOK], ALU.add).then_inc(sumsq_step, 1)

        def sum_all(n):
            sum_squares(n, 0, 0, True)
            for k in range(1, 4):
                sum_squares(n, k, k % 2, False)
            with pool.Fori(1, KT // 4) as i:
                for q in range(4):
                    sum_squares(n, i * 4 + q, q % 2, False)

        for k in range(KT):
            sum_squares(0, k, k % 2, k == 0)
        pool.wait_ge(rel_built, 3)
        pool.dma_start(rel_dram, rel_u[:].to_broadcast((HA, P, 640))).then_inc(rel_stored, 16)
        pool.wait_ge(rel_stored, 16)

        pool.wait_ge(qk_norm, 10)
        pool.wait_ge(lr_done, 1)
        pool.dma_start(ck_rows[:], cache_a_k[0, 0].rearrange("(a p) h d -> p a (h d)", p=P)).then_inc(late_landed, 16)
        pool.dma_start(cv_rows[:], cache_a_v[0, 0].rearrange("(a p) h d -> p a (h d)", p=P)).then_inc(late_landed, 16)

        def load_bias(h):
            src = bass.AP(tensor=rel_dram.tensor, offset=h * P * 640 + P - 1, ap=[[640 - 1, P], [1, 512]])
            pool.dma_start(bias[:, h % 2, :], src).then_inc(bias_landed, 16)
            pool.wait_ge(bias_landed, 16 * (h + 1))
            pool.memset(bias[0:CHUNK, h % 2, 512 - CHUNK:512], NEG).then_inc(bias_ready, 1)

        load_bias(0)
        load_bias(1)
        pool.wait_ge(rows_out[0], 8)
        pool.wait_ge(rows_out[1], 7)
        for rows, prompt, sample in ((k_rows, ak_prompt, ak_sample), (v_rows, av_prompt, av_sample)):
            pool.dma_start(prompt[0, 0].rearrange("(c p) h d -> p c (h d)", p=P), rows[:, 0:TT, :])\
                .then_inc(stored, 16)
            pool.dma_start(sample[0, 0].rearrange("t h d -> t (h d)"), rows[0:DEC, TT, :]).then_inc(stored, 16)
        for h in range(2, HA):
            pool.wait_ge(score_read, 5 * (h - 1))
            load_bias(h)
        pool.wait_ge(state_ready, 20)
        pool.dma_start(sb_prompt[0, 0].rearrange("(a b) k v -> (b k) a v", b=2), state[:]).then_inc(stored, 16)
        pool.dma_start(sb_sample[0, 0].rearrange("(a b) k v -> (b k) a v", b=2), state_s[:]).then_inc(stored, 16)

        sum_all(1)
        sum_all(2)
        pool.wait_ge(gemm_done, tile0(U_PW1))
        pool.memset(glu[:, :, 0:PAD], 0.0).then_inc(glu_edges, 1)
        pool.tensor_copy(glu[:, :, PAD + SEQ:PAD + SEQ + PAD], cc_T[:]).then_inc(glu_edges, 1)
        pool.memset(glu[:, :, FW - 2:FW], 0.0).then_inc(glu_edges, 1)
        pool.wait_ge(slot_free[0], tile0(U_PW2) // 2)
        pool.wait_ge(slot_free[1], tile0(U_PW2) // 2)
        pool.dma_start(cc_prompt[0, 0], ccn[:, 0, :]).then_inc(stored, 16)
        pool.dma_start(cc_sample[0, 0], ccn[:, 1, :]).then_inc(stored, 16)
        sum_all(3)
        pool.wait_ge(stored, 16 * 8)

    @block.scalar
    def _(act):
        steps = [0]

        def own(ins):
            ins.then_inc(a_step, 1)
            steps[0] += 1
            act.wait_ge(a_step, steps[0])

        rows = lambda v: v.rearrange("a (r p) -> (a r) p", p=P)
        for at, n, src in ((V_MIX, 16, rows(norm_mix_g)), (V_FFN, 16, rows(norm_ffn_g))):
            act.dma_start(vec_rows[at:at + n, :], src).then_inc(gains_landed, 16)
        for at, n, src in ((V_B1, 16, rows(c_b_pw1)), (V_BDW, 8, rows(c_b_dw)), (V_LNG, 8, rows(c_ln_g)),
                           (V_LNB, 8, rows(c_ln_b)), (V_B2, 8, rows(c_b_pw2)), (V_GB, 2, rows(b_gate_b)),
                           (V_ON, 1, b_out_norm_g)):
            act.dma_start(vec_rows[at:at + n, :], src).then_inc(rows_landed, 16)
        for at, src in ((V_QG, a_q_norm_g), (V_KG, a_k_norm_g)):
            for b in range(2):
                act.dma_start(vec_rows[at:at + 1, b * DA:(b + 1) * DA], src).then_inc(rows_landed, 16)
        act.dma_start(wlr[:], w_view(w_in_ab[0])[:, :, N_PROJ * P:N_PROJ * P + RANK]).then_inc(rows_landed, 16)
        act.dma_start(dw_rows[:], c_w_dw[0]).then_inc(rows_landed, 16)
        act.dma_start(cc_rows[:], cache_c[0, 0]).then_inc(rows_landed, 16)
        act.dma_start(gate_w[:], b_gate_w_up[0]).then_inc(rows_landed, 16)
        act.dma_start(rel[:], a_rel_bias[0]).then_inc(rows_landed, 16)
        act.dma_start(state_s[:], state_b[0, 0].rearrange("(a b) k v -> (b k) a v", b=2)).then_inc(rows_landed, 16)

        def split_hi(u, i, d):
            s = d % 2
            act.wait_ge(w_landed[s], i * 16 + 16 * (u // 2 + d // 2 + 1))
            if not (u == 0 and isinstance(i, int) and i == 0 and d < 2):
                act.wait_ge(gemm_done, i * 2 * 2 + (tile0(u + d - 2) + 2))
            act.activation(w_h[:, s], w_raw[:, s], ACT.Copy).then_inc(w_hi, 1)

        def phase(u0, units, evacuate, first=None):
            if first:
                for s in range(2):
                    split_hi(u0, 0, s + 1)
                    if s == 0:
                        first()
                    evacuate(0, s)
            with act.Fori(1 if first else 0, units // 2) as i:
                for s in range(2):
                    split_hi(u0, i, s + 1)
                    evacuate(i, s)

        def square(n, k, parity, ready, at):
            act.wait_ge(ready, at)
            if not (n == 0 and isinstance(k, int) and k < 2):
                act.wait_ge(sumsq_step, k + (8 * n - 1))
            act.activation(sq[:, parity, 0:TOK], resid_tile(k), ACT.Square).then_inc(sq_ready, 1)

        def resid_tile(k):
            return resid[:, k, :] if isinstance(k, int) else \
                resid[:, bass.ds(k, 1), :].rearrange("p o t -> p (o t)")

        def hi_gain(x0, xh, k, gain, ready, at):
            act.wait_ge(ready, at)
            act.activation(xh[:, k, :] if isinstance(k, int) else
                           xh[:, bass.ds(k, 1), :].rearrange("p o t -> p (o t)"), resid_tile(k), ACT.Copy,
                           scale=vecs[:, bass.ds(k + gain, 1)]).then_inc(xh_ready, 1)

        def frame_std(n):
            act.wait_ge(ms_ready, n + 1)
            act.activation(halves(sumsq[:]), sum_ps(0), ACT.Sqrt, bias=eps[:, 0:1]).then_inc(std_ready, 1)

        act.wait_ge(consts, 1)
        act.wait_ge(gains_ready, 1)
        for k in range(KT):
            hi_gain(0, x_h, k, V_MIX, slot_free[k % 2], k // 2 + 1)
            if k == 1:
                split_hi(0, 0, 0)
            square(0, k, k % 2, slot_free[k % 2], k // 2 + 1)
        act.wait_ge(vec_ready, 1)
        act.activation(w_dw_h[:], w_dw[:, :, 0:PE_TAPS], ACT.Copy).then_inc(w_dw_hi, 1)
        act.activation(wlr_h[:, :, 0:RANK], wlr[:], ACT.Copy).then_inc(wlr_hi, 1)

        def norm(n, x0):
            frame_std(n)
            for k in range(KT):
                act.wait_ge(xn_ready, k + 1)
                act.activation(x_h[:, k, :], xn[:, k % 3, :], ACT.Copy).then_inc(xh_ready, 1)

        def squares_qk(i, s):
            for m in range(2):
                t = i * 4 + (2 * s + m)
                act.wait_ge(slot_free[m], i * 2 + (tile0(s) // 2 + 1))
                act.activation(qk_sq[:, bass.ds(t, 1), :], proj[:, bass.ds(t, 1), :], ACT.Square)\
                    .then_inc(qk_sq_ready, 1)

        def std_qk(i, s):
            act.wait_ge(qk_ms, i * 2 + (s + 1))
            act.wait_ge(qk_norm, i * 2 + (s + 2))
            act.activation(halves(sumsq[:]), sum_ps(s), ACT.Sqrt, bias=eps[:, 0:1]).then_inc(qk_std, 1)

        def before_squares():
            frame_std(0)
            act.wait_ge(rel_stored, 16)

        phase(0, 4, squares_qk, first=before_squares)
        phase(4, 6, std_qk)
        split_hi(10, 0, 1)
        std_qk(3, 0)
        std_qk(3, 1)

        act.wait_ge(slot_free[1], tile0(U_OUT) // 2)
        act.activation(proj[:, T_GB:T_GB + 4, :], proj[:, T_GB:T_GB + 4, :], ACT.Silu).then_inc(silu_done, 1)

        for g in range(0, 17, 2):
            act.wait_ge(rows_T, g + 1)
            dst, src = rows_group(g)
            act.activation(dst, src, ACT.Copy).then_inc(rows_out[0], 1)

        for n in range(2):
            act.wait_ge(gate_done, n + 1)
            if n:
                act.wait_ge(gate_ln, 2)
            own(act.activation(halves(gl_a), sum_ps(n), ACT.Abs, bias=vecs[:, V_GB + n:V_GB + n + 1]))
            act.activation(gl_a, gl_a, ACT.Exp, scale=-1.0).then_inc(gate_abs, 1)
            act.wait_ge(gate_abs, n + 1)
            act.activation(gl_a, gl_a, ACT.Ln, bias=1.0).then_inc(gate_ln, 1)
            act.wait_ge(gate_ln, 2 * n + 2)
        for n in range(2):
            act.wait_ge(bt_ready, 5 * (n + 1))
            act.activation(eb[:, n, :], bt[:, n, :], ACT.Exp, scale=1.0 / 16).then_inc(eb_ready, 1)

        def exp_scores(n):
            M, nk = width(n % 5), keys(n)
            act.wait_ge(nmax_ready, n + 1)
            act.activation(prob[0:M, n % 4, 0:nk], prob[0:M, n % 4, 0:nk], ACT.Exp, bias=small[0:M, 4 + n % 4:5 + n % 4],
                           accum_out=small[0:M, 8 + n % 4:9 + n % 4]).then_inc(exp_done, 1)

        def copy_probT(n):
            M, nk = width(n % 5), keys(n)
            act.wait_ge(probT_done, n + 1)
            if n >= 2:
                act.wait_ge(o_done, n - 1)
            full = nk // P * M
            ins = act.activation(prob_T[:, n % 2, 0:full], ps[:, 2 + n % 2, 0:full], ACT.Copy)
            if nk % P:
                ins = act.activation(prob_T[0:nk % P, n % 2, full:full + M], ps[0:nk % P, 2 + n % 2, full:full + M],
                                     ACT.Copy)
            ins.then_inc(probT_ready, 1)

        def copy_o(n):
            h, c = n // 5, n % 5
            b = h % 2 * DA
            act.wait_ge(o_done, n + 1)
            act.activation(proj[b:b + DA, T_Q + h // 2, frames(c)], ps[b:b + DA, 4 + n % 2, 0:width(c)],
                           ACT.Copy).then_inc(o_copied, 1)

        def exp_decays(n):
            if 6 <= n < 8:
                act.wait_ge(kd_diff, n - 5)
                act.activation(kd[:, n - 6, :], kd[:, n - 6, :], ACT.Exp, scale=1.0 / 16).then_inc(kd_exp, 1)
            if 8 <= n < 22 and n % 2 == 0:
                l = (n - 8) // 2
                cols = slice(0, SEQ if l < 2 else TOK)
                act.wait_ge(lev_diff, 2 * (l + 1))
                act.activation(lev[:, l, :, cols], lev[:, l, :, cols], ACT.Exp, scale=1.0 / 16).then_inc(lev_exp, 1)

        for t in range(5 * HA + 6):
            if t >= 6:
                copy_o(t - 6)
            if 4 <= t < 5 * HA + 4:
                copy_probT(t - 4)
            if 1 <= t < 5 * HA + 1:
                exp_scores(t - 1)
                exp_decays(t - 1)

        for n in range(2):
            act.wait_ge(kd_T, n + 1)
            src = kd_bank(n)
            act.activation(kd_rows[:, 0:TT, n * P:(n + 1) * P], ps[:, src, :].rearrange("p (c f) -> p c f", f=P),
                           ACT.Copy)
            act.activation(kd_rows[0:DEC, TT, n * P:(n + 1) * P], ps[0:DEC, src + 1, 0:P], ACT.Copy)\
                .then_inc(kd_rows_ready, 1)
        for m in range(20):
            h, c = 2 * (m // 10) + m % 2, m % 10 // 2
            act.wait_ge(ob_done, m + 1)
            act.activation(proj[:, T_VB + h, frames(c)], ps[:, 4 + m % 2, 0:width(c)], ACT.Copy)\
                .then_inc(ob_ready, 1)
        split_hi(U_OUT, 0, 0)
        for h in range(HB):
            if h == 0:
                act.wait_ge(ob_ready, 20)
            if h >= 2:
                act.wait_ge(ob_ms, h - 1)
            act.activation(sq[:, h % 2, 0:TOK], proj[:, T_VB + h, :], ACT.Square).then_inc(ob_sq, 1)
            if h >= 1:
                ob_root(act, h - 1)
        ob_root(act, HB - 1)
        for k in range(KT):
            if k < 4:
                if k == 0:
                    act.wait_ge(ob_done, 20)
                    act.wait_ge(state_ready, 20)
                    act.wait_ge(stored, 16 * 4)
                src = proj[:, T_Q + k, :]
            else:
                act.wait_ge(ob_cat, k - 3)
                src = proj[:, T_VB + k - 4, :]
            act.activation(x_h[:, k, :], src, ACT.Copy).then_inc(xh_ready, 1)

        def squares_of(n, u0, gain=None):
            def evacuate(i, s):
                for m in range(2):
                    k, at = i * 4 + (2 * s + m), i * 2 + (tile0(u0 + s) // 2 + 1)
                    square(n, k, m, slot_free[m], at)
                    if gain is not None:
                        hi_gain(n, xf_h, k, gain, slot_free[m], at)
            return evacuate

        phase(U_OUT, 4, squares_of(1, U_OUT, V_FFN))

        def hidden(layer, c, u0):
            base = 4 * 8 * layer + 8 * c

            def evacuate(i, s):
                for m in range(2):
                    act.wait_ge(slot_free[m], i * 2 + (tile0(u0 + s) // 2 + 1))
                    act.activation(relu2[:, m, :], relu[:, m, :], ACT.Square).then_inc(relu2_done, 1)
                    act.wait_ge(relu2_done, i * 4 + (base + 2 * s + m + 1))
                    act.activation(hid_h[c % 2][:, bass.ds(i * 4 + (2 * s + m), 1), :].rearrange("p o t -> p (o t)"),
                                   relu2[:, m, :], ACT.Copy).then_inc(hidh_done, 1)
            return evacuate

        def ffn(layer, u0, last):
            for n, (way, c) in enumerate(FFN_ORDER):
                u = u0 + 4 * n
                if way == "up":
                    phase(u, 4, hidden(layer, c, u), first=(lambda: frame_std(2 * layer + 1)) if c == 0 else None)
                elif c < NF - 1:
                    phase(u, 4, lambda i, s: None)
                else:
                    last(u)

        ffn(0, U_FFN0, lambda u: phase(u, 4, squares_of(2, u)))
        norm(2, X_MIX1)

        def gate(i, s):
            m = i * 2 + s
            act.wait_ge(gemm_done, i * 4 + (tile0(U_PW1 + s) + 1))
            act.activation(halves(sig[:, s, :]), slot(0), ACT.Sigmoid,
                           bias=vecs[:, bass.ds(i * 2 + (V_B1 + 8 + s), 1)]).then_inc(slot_free[0], 1)
            act.wait_ge(taps_done, m + 1)
            act.wait_ge(slot_free[1], m + (tile0(U_PW1) // 2 + 1))
            act.activation(glu_h[:, s, :], glu[:, bass.ds(m, 1), :].rearrange("p o t -> p (o t)"), ACT.Copy)\
                .then_inc(glu_hi, 1)

        def diagonals(i, s):
            m = i * 2 + s
            for t in range(PE_TAPS):
                for part, w in ((diag_h, w_dw_h[:].bitcast(F32)), (diag_l, w_dw_l[:])):
                    w = w.rearrange("p k c -> p (k c)")
                    ins = act.activation(part[:, s, t, :], ident[:], ACT.Identity,
                                         scale=w[:, bass.ds(m * PE_TAPS + t, 1)])
            ins.then_inc(diag_ready, 1)

        act.wait_ge(w_dw_lo, 1)
        act.wait_ge(glu_edges, 3)
        split_hi(U_PW1, 0, 1)
        with act.Fori(0, KT // 2 - 1) as i:
            for s in range(2):
                gate(i, s)
                split_hi(U_PW1, i, s + 2)
                diagonals(i, s)
        gate(KT // 2 - 1, 0)
        split_hi(U_PW1, KT // 2 - 1, 2)
        diagonals(KT // 2 - 1, 0)
        gate(KT // 2 - 1, 1)
        diagonals(KT // 2 - 1, 1)
        act.wait_ge(taps_done, KT + 2)
        act.wait_ge(gemm_done, tile0(U_PW2) - 1)
        act.activation(ccn[:, 0, :], flat(0)[0:PAD, :], ACT.Copy).then_inc(slot_free[0], 1)
        for k in range(KT):
            act.wait_ge(cv_centred, k + 1)
            if k >= 2:
                act.wait_ge(cv_var, k - 1)
            act.activation(sq[:, k % 2, :], cv[:, k, :], ACT.Square).then_inc(cv_sq, 1)
        act.wait_ge(cv_var, KT)
        act.activation(rstd[:].rearrange("p (a t) -> p a t", a=2), sum_ps(1, CW // 2), ACT.Sqrt,
                       bias=eps[:, 0:1]).then_inc(cv_std, 1)
        for k in range(KT):
            act.wait_ge(cv_norm, k + 1)
            if k >= 3:
                act.wait_ge(xl_ready, X_PW2 + k - 2)
            for to, of in ((slice(0, SEQ), slice(0, SEQ)), (slice(SEQ, TOK), slice(SEQ + PAD, SEQ + PAD + DEC))):
                ins = act.activation(xn[:, k % 3, to], cv[:, k, of], ACT.Silu, scale=vecs[:, V_LNG + k:V_LNG + k + 1],
                                     bias=vecs[:, V_LNB + k:V_LNB + k + 1])
            ins.then_inc(cv_silu, 1)
            act.wait_ge(cv_silu, k + 1)
            act.activation(x_h[:, k, :], xn[:, k % 3, :], ACT.Copy).then_inc(xh_ready, 1)
        act.wait_ge(stored, 16 * 8)
        phase(U_PW2, 4, squares_of(3, U_PW2, V_FFN + 8))

        def y_out(u):
            for i in range(2):
                for s in range(2):
                    if u + 2 * i + s + 1 < U_END:
                        split_hi(u, i, s + 1)
                    for m in range(2):
                        k = 4 * i + 2 * s + m
                        act.wait_ge(y_T, k + 1)
                        if k >= 2:
                            act.wait_ge(y_stored[k % 2], 32 * (k // 2))
                        b = sum_flat(k % 2)
                        act.activation(y_rows[:, k % 2, 0:TT, :], b[:, 0:SEQ].rearrange("p (c f) -> p c f", f=P),
                                       ACT.Copy).then_inc(y_stage, 1)
                        act.activation(y_rows[0:DEC, k % 2, TT, :], b[0:DEC, 512:512 + P], ACT.Copy)\
                            .then_inc(y_stage, 1)

        ffn(1, U_FFN1, y_out)

    @block.tensor
    def _(pe):
        pe.wait_ge(gains_landed, 32)
        pe.wait_ge(consts, 1)
        pe.transpose(ps[:, 4, 0:V_B1], vec_rows[0:V_B1, :], ident[0:V_B1, 0:V_B1]).then_inc(gains_T, 1)
        for k in range(KT):
            if k >= 2:
                pe.wait_ge(slot_free[k % 2], k // 2)
            for c in range(TT + 1):
                if k == 0:
                    pe.wait_ge(x_landed[c], 16)
                M = width(c)
                ins = pe.transpose(flat(k % 2)[:, c * P:c * P + M], x_rows[0:M, c, k * P:(k + 1) * P],
                                   ident[0:M, 0:M])
            ins.then_inc(gemm_done, 1)
        pe.wait_ge(rows_landed, 16 * 17)
        pe.transpose(ps[:, 7, 0:V_N], vec_rows[:], ident[0:V_N, 0:V_N]).then_inc(vec_T, 1)
        for k in range(KT):
            ins = pe.transpose(ps[:, 5, k * CONV:(k + 1) * CONV], dw_rows[:, k * P:(k + 1) * P], ident[0:CONV, 0:CONV])
        ins.then_inc(vec_T, 1)
        for k in range(KT):
            ins = pe.transpose(ps[:, 6, k * PAD:(k + 1) * PAD], cc_rows[:, k * P:(k + 1) * P], ident[0:PAD, 0:PAD])
        ins.then_inc(vec_T, 1)

        def mean_of(dst, src, w, n=HALF, start=True, stop=True):
            for a in range(2):
                ins = pe.matmul(dst[:, a, :], w[:], src[:, a * n:(a + 1) * n], start=start, stop=stop)
            return ins

        def norm(n):
            pe.wait_ge(sumsq_step, 8 * (n + 1))
            mean_of(sum_ps(0), sumsq, mean_d).then_inc(ms_ready, 1)

        def tile(s, m, xh, xl, ready=None):
            for k in range(KT):
                if ready:
                    ready(k)
                w = slice(m * P, (m + 1) * P)
                for q, (a, b) in enumerate(((w_h, xh), (w_h, xl), (w_l, xh))):
                    for t in range(2):
                        ins = pe.matmul(ps[:, 2 * m + t, 0:HALF], a[:, s, k, w], b[:, k, t * HALF:(t + 1) * HALF],
                                        start=(k == 0 and q == 0), stop=(k == KT - 1 and q == 2))
            ins.then_inc(gemm_done, 1)

        def unit(u0, i, s, xh, xl, ready=None, between=None):
            pe.wait_ge(w_lo, i * 2 + (u0 + s + 1))
            for m in range(2):
                pe.wait_ge(slot_free[m], i * 2 + tile0(u0 + s) // 2)
                tile(s, m, xh, xl, ready if s == 0 and m == 0 else None)
                if between and m == 0:
                    between()

        def project(u0, units, xh, xl, x0=None, before=lambda i, s: None, after=lambda i, s: None, between=None):
            ready = None if x0 is None else (lambda k: pe.wait_ge(xl_ready, x0 + k + 1))
            if between:
                unit(u0, 0, 0, xh, xl, ready, between)
                unit(u0, 0, 1, xh, xl)
                ready = None
            with pe.Fori(1 if between else 0, units // 2) as i:
                for s in range(2):
                    before(i, s)
                    unit(u0, i, s, xh, xl, ready)
                    after(i, s)

        def mean_square():
            pe.wait_ge(vec_ready, 1)
            norm(0)

        project(0, 4, x_h, x_l, X_MIX0, between=mean_square)

        def qk_mean(i, s):
            pe.wait_ge(qk_sq_ready, 8)
            pe.wait_ge(qk_norm, i * 2 + (s + 1))
            src = qk_sq[:, bass.ds(i * 2 + s, 1), :].rearrange("p o t -> p (o t)")
            mean_of(sum_ps(s), src, mean_ha).then_inc(qk_ms, 1)

        project(4, 8, x_h, x_l, before=qk_mean)
        pe.wait_ge(wlr_lo, 1)
        pe.wait_ge(qk_std, 8)
        for k in range(KT):
            for q, (a, b) in enumerate(((wlr_h, x_h), (wlr_h, x_l), (wlr_l, x_h))):
                for t in range(2):
                    ins = pe.matmul(ps[:, 4 + t, 0:HALF], a[:, k, :], b[:, k, t * HALF:(t + 1) * HALF],
                                    start=(k == 0 and q == 0), stop=(k == KT - 1 and q == 2))
        ins.then_inc(lr_done, 1)
        pe.wait_ge(slot_free[0], tile0(U_OUT) // 2)
        pe.wait_ge(slot_free[1], tile0(U_OUT) // 2)
        pe.wait_ge(qk_norm, 10)
        for g in range(17):
            if g >= 4:
                pe.wait_ge(rows_out[g % 2], (g - 4) // 2 + 1)
            if g == 15:
                pe.wait_ge(late_landed, 32)
            for n in range(4):
                if g < 15:
                    c = g // 3
                    src = proj[:, (T_K, T_V, T_VB)[g % 3] + n, frames(c)]
                    ins = pe.transpose(ps[0:width(c), g % 4, n * P:(n + 1) * P], src, ident[:])
                else:
                    f = 2 * (g - 15) + n // 2
                    ins = pe.transpose(ps[:, g % 4, n * P:(n + 1) * P], ck_rows[:, n % 2, f * P:(f + 1) * P], ident[:])
            ins.then_inc(rows_T, 1)
        pe.wait_ge(lr_ready, 1)
        for n in range(2):
            mean_of(sum_ps(n), lr, gate_w[:, n * P:(n + 1) * P]).then_inc(gate_done, 1)

        def scores(n):
            h, c = n // 5, n % 5
            b, M = h % 2 * DA, width(c)
            if n >= 2:
                pe.wait_ge(score_read, n - 1)
            q = proj[b:b + DA, T_Q + h // 2, frames(c)]
            k = proj[b:b + DA, T_K + h // 2, :]
            if c < TT:
                ins = pe.matmul(ps[0:M, n % 2, 0:keys(n)], q, k[:, 0:keys(n)], start=True, stop=True)
            else:
                pe.matmul(ps[0:M, n % 2, 0:PAST], q, ck_T[b:b + DA, h // 2, :], start=True, stop=True)
                ins = pe.matmul(ps[0:M, n % 2, PAST:PAST + DEC], q, k[:, SEQ:TOK], start=True, stop=True)
            ins.then_inc(score_done, 1)

        def key_tiles(n):
            return [(j, min(P, keys(n) - j * P)) for j in range((keys(n) + P - 1) // P)]

        def turn(n):
            M = width(n % 5)
            pe.wait_ge(prob_ready, n + 1)
            if n >= 2:
                pe.wait_ge(probT_ready, n - 1)
            for j, w in key_tiles(n):
                ins = pe.transpose(ps[0:w, 2 + n % 2, j * M:(j + 1) * M], prob[0:M, n % 4, j * P:j * P + w],
                                   ident[0:M, 0:M])
            ins.then_inc(probT_done, 1)

        def values(n):
            h, c = n // 5, n % 5
            b, M = h % 2 * DA, width(c)
            pe.wait_ge(probT_ready, n + 1)
            if n >= 2:
                pe.wait_ge(o_copied, n - 1)
            tiles = key_tiles(n)
            for j, w in tiles:
                rows = v_rows[0:w, j, :] if c < TT else (cv_rows[:, j, :] if j < 2 else v_rows[0:w, TT, :])
                ins = pe.matmul(ps[b:b + DA, 4 + n % 2, 0:M], rows[:, h * DA:(h + 1) * DA],
                                prob_T[0:w, n % 2, j * M:(j + 1) * M], start=(j == 0), stop=(j == len(tiles) - 1))
            ins.then_inc(o_done, 1)

        pe.wait_ge(rows_out[0], 9)
        pe.wait_ge(rows_out[1], 8)
        pe.wait_ge(gate_min, 2)
        for t in range(5 * HA + 5):
            if t < 5 * HA:
                scores(t)
            if 3 <= t < 5 * HA + 3:
                turn(t - 3)
            if t >= 5:
                values(t - 5)

        pe.wait_ge(o_copied, 5 * HA)
        for n in range(2):
            pe.wait_ge(kd_ready, n + 1)
            for c in range(TT + 1):
                M = width(c)
                dst = ps[0:M, kd_bank(n), c * P:(c + 1) * P] if c < TT else ps[0:M, kd_bank(n) + 1, 0:P]
                ins = pe.transpose(dst, kd[:, n, frames(c)], ident[:])
            ins.then_inc(kd_T, 1)

        def head_of(m):
            return 2 * (m // 10) + m % 2, m % 10 // 2, m % 2 * DKB

        def pairs(m):
            h, c, b = head_of(m)
            M = width(c)
            if m == 0:
                pe.wait_ge(lev_ready, 1)
            if m >= 2:
                pe.wait_ge(masked_done, m - 1)
            for n in range(0 if c < TT else 2, 8):
                l = lev[b:b + DKB, n, h // 2, frames(c)] if n < 7 else proj[b:b + DKB, T_KB + h // 2, frames(c)]
                r = l if n < 7 else proj[b:b + DKB, T_QB + h // 2, frames(c)]
                at = 2 * (m % 2) + n // 4
                ins = pe.matmul(ps[0:M, at, n % 4 * P:n % 4 * P + M], l, r, start=True, stop=True)
            ins.then_inc(pairs_done, 1)

        def outputs(m):
            h, c, b = head_of(m)
            M = width(c)
            if m >= 2:
                pe.wait_ge(state_ready, m - 1)
            pe.matmul(ps[b:b + DKB, 6 + m % 2, 0:DVB], kd_rows[0:M, c, h * DKB:(h + 1) * DKB],
                      vb_rows[0:M, c, h * DVB:(h + 1) * DVB], start=True, stop=True).then_inc(kv_done, 1)
            pe.wait_ge(pair_ready, m + 1)
            if m >= 2:
                pe.wait_ge(ob_ready, m - 1)
            o = ps[:, 4 + m % 2, 0:M]
            ins = pe.matmul(o, vb_rows[0:M, c, h * DVB:(h + 1) * DVB], pair[0:M, m % 2, 0:M], start=True, stop=(c == 0))
            if c:
                st = state if c < TT else state_s
                ins = pe.matmul(o, st[b:b + DKB, h // 2, :], qe[b:b + DKB, h // 2, frames(c)], start=False, stop=True)
            ins.then_inc(ob_done, 1)

        pairs(0)
        pe.wait_ge(kd_rows_ready, 2)
        for m in range(20):
            if m + 1 < 20:
                pairs(m + 1)
            outputs(m)
        for h in range(HB):
            pe.wait_ge(ob_sq, h + 1)
            if h == 0:
                pe.wait_ge(state_ready, 20)
            if h >= 2:
                pe.wait_ge(ob_std, h - 1)
            mean_of(sum_ps(h % 2), sq[:, h % 2, :], mean_hb).then_inc(ob_ms, 1)

        pe.wait_ge(ob_std, HB)
        project(U_OUT, 4, x_h, x_l, X_CAT)

        def ffn(layer, u0, x0, last):
            for n, (way, c) in enumerate(FFN_ORDER):
                u = u0 + 4 * n
                if way == "up":
                    if c == 0:
                        project(u, 4, xf_h, xf_l, x0, between=lambda: norm(2 * layer + 1))
                    else:
                        project(u, 4, xf_h, xf_l)
                    continue
                pe.wait_ge(hidl_done, 2 + 32 * layer + 8 * (c + 1))
                if c < NF - 1:
                    project(u, 4, hid_h[c % 2], hid_l[c % 2])
                else:
                    last(u, hid_h[c % 2], hid_l[c % 2])

        ffn(0, U_FFN0, X_FFN0, lambda u, h, l: project(u, 4, h, l))
        norm(2)

        def gated(i, d):
            s = d % 2
            pe.wait_ge(w_lo, i * 2 + (U_PW1 + d + 1))
            for m in range(2):
                pe.wait_ge(slot_free[m], i * 2 + tile0(U_PW1 + d) // 2)
                first = isinstance(i, int) and i + d + m == 0
                tile(s, m, x_h, x_l, (lambda k: pe.wait_ge(xl_ready, X_MIX1 + k + 1)) if first else None)

        def add_taps(i, d):
            m, s = i * 2 + d, d % 2
            pe.wait_ge(diag_ready, m + 1)
            pe.wait_ge(glu_lo, m + 1)
            pe.wait_ge(conv_ready, m + 1)
            for t in range(PE_TAPS):
                for q, (a, b) in enumerate(((diag_h, glu_h), (diag_h, glu_l), (diag_l, glu_h))):
                    for c in range(2):
                        at = t + c * (CW // 2)
                        ins = pe.matmul(sum_ps(1, CW // 2)[:, c, :], a[:, s, t, :], b[:, s, at:at + CW // 2],
                                        start=(t == 0 and q == 0), stop=(t == PE_TAPS - 1 and q == 2))
            ins.then_inc(taps_done, 1)

        def add_mean(i, d, start=False, stop=False):
            pe.wait_ge(conv_ready, i * 2 + (d + 2))
            src = cv[:, bass.ds(i * 2 + d, 1), :].rearrange("p o t -> p (o t)")
            return mean_of(sum_ps(0, CW // 2), src, mean_d, CW // 2, start, stop)

        gated(0, 0)
        gated(0, 1)
        add_taps(0, 0)
        gated(0, 2)
        add_taps(0, 1)
        add_mean(0, 0, start=True)
        with pe.Fori(1, KT // 2 - 1) as i:
            for s in range(2):
                gated(i, s + 1)
                add_taps(i, s)
                add_mean(i, s - 1)
        gated(KT // 2 - 1, 1)
        add_taps(KT // 2 - 1, 0)
        add_mean(KT // 2 - 1, -1)
        for n in range(2):
            pe.wait_ge(slot_free[n], tile0(U_PW2) // 2 - 1)
        for n in range(2):
            at = SEQ if n == 0 else SEQ + PAD + DEC
            for k in range(KT):
                ins = pe.transpose(flat(n)[0:PAD, k * P:(k + 1) * P], glu[:, k, at:at + PAD], ident[:])
            ins.then_inc(gemm_done, 1)
        add_taps(KT // 2 - 1, 1)
        add_mean(KT // 2 - 1, 0)
        add_mean(KT // 2 - 1, 1, stop=True).then_inc(cvmean, 1)
        for k in range(KT):
            pe.wait_ge(cv_sq, k + 1)
            mean_of(sum_ps(1, CW // 2), sq[:, k % 2, :], mean_d, CW // 2, k == 0, k == KT - 1).then_inc(cv_var, 1)
        project(U_PW2, 4, x_h, x_l, X_PW2)

        def last_down(u, h, l):
            def rows_of(k):
                pe.wait_ge(y_ready, k + 1)
                if k >= 2:
                    pe.wait_ge(y_stage, 2 * (k - 1))
                for c in range(TT + 1):
                    ins = pe.transpose(sum_flat(k % 2)[0:width(c), c * P:(c + 1) * P], y_fin[:, k % 2, frames(c)],
                                       ident[:])
                ins.then_inc(y_T, 1)

            for i in range(2):
                for s in range(2):
                    pe.wait_ge(w_lo, u + 2 * i + s + 1)
                    for m in range(2):
                        k = 4 * i + 2 * s + m
                        pe.wait_ge(slot_free[m], tile0(u + 2 * i + s) // 2)
                        tile(s, m, h, l)
                        if k >= 1:
                            rows_of(k - 1)
            rows_of(KT - 1)

        ffn(1, U_FFN1, X_FFN1, last_down)

    @block.vector
    def _(dve):
        steps = [0]

        def own(ins):
            ins.then_inc(v_step, 1)
            steps[0] += 1
            dve.wait_ge(v_step, steps[0])

        dve.engine_nop().then_inc(hidl_done, 2)
        dve.engine_nop().then_inc(qk_norm, 2)
        dve.engine_nop().then_inc(conv_ready, 1)
        dve.engine_nop().then_inc(taps_done, 2)
        dve.wait_ge(gains_T, 1)
        dve.tensor_copy(vecs[:, 0:V_B1], ps[:, 4, 0:V_B1]).then_inc(gains_ready, 1)
        dve.wait_ge(gains_ready, 1)

        def split_lo(u, i, d):
            s = d % 2
            dve.wait_ge(w_hi, i * 2 + (u + d + 1))
            dve.tensor_tensor(w_l[:, s], w_raw[:, s], w_h[:, s].bitcast(F32), ALU.subtract).then_inc(w_lo, 1)

        def phase(u0, units, evacuate, first=None):
            if first:
                for s in range(2):
                    split_lo(u0, 0, s + 1)
                    if s == 0:
                        first()
                    evacuate(0, s)
            with dve.Fori(1 if first else 0, units // 2) as i:
                for s in range(2):
                    split_lo(u0, i, s + 1)
                    evacuate(i, s)

        def lo_gain(k, x0, xl, xh, gain):
            dve.wait_ge(xh_ready, k + (x0 + 1))
            r, l, h = at(resid, k), at(xl, k), at(xh, k).bitcast(F32)
            dve.scalar_tensor_tensor(out=l, in0=r, scalar=vecs[:, bass.ds(k + gain, 1)], in1=h,
                                     op0=ALU.mult, op1=ALU.subtract).then_inc(xl_ready, 1)

        def frame_scale(n):
            dve.wait_ge(std_ready, n + 1)
            dve.reciprocal(r_tok, sumsq[:]).then_inc(r_ready, 1)
            dve.wait_ge(r_ready, (n + 3) // 2)

        def lo(k, x0, src):
            dve.wait_ge(xh_ready, x0 + k + 1)
            dve.tensor_tensor(x_l[:, k, :], src, x_h[:, k, :].bitcast(F32), ALU.subtract).then_inc(xl_ready, 1)

        def norm(n, x0, gain):
            dve.wait_ge(std_ready, n + 1)
            own(dve.reciprocal(rstd[:, 0:TOK], sumsq[:]))
            for k in range(KT + 1):
                if k < KT:
                    if k >= 3:
                        dve.wait_ge(xl_ready, x0 + k - 2)
                    dve.scalar_tensor_tensor(out=xn[:, k % 3, :], in0=resid[:, k, :],
                                             scalar=vecs[:, gain + k:gain + k + 1], in1=rstd[:, 0:TOK],
                                             op0=ALU.mult, op1=ALU.mult).then_inc(xn_ready, 1)
                if k >= 1:
                    lo(k - 1, x0, xn[:, (k - 1) % 3, :])

        def at(tensor, t):
            return tensor[:, t, :] if isinstance(t, int) else tensor[:, bass.ds(t, 1), :].rearrange("p o t -> p (o t)")

        for k in range(KT + 1):
            if k < KT:
                dve.wait_ge(gemm_done, k + 1)
                dve.tensor_copy(resid[:, k, :], flat(k % 2)[:, 0:TOK]).then_inc(slot_free[k % 2], 1)
            if k == 2:
                split_lo(0, 0, 0)
            if k:
                dve.wait_ge(slot_free[(k - 1) % 2], (k + 1) // 2)
                lo_gain(k - 1, X_MIX0, x_l, x_h, V_MIX)
        dve.wait_ge(vec_T, 1)
        own(dve.tensor_copy(vecs[:, V_B1:V_N], ps[:, 7, V_B1:V_N]))
        for k in range(4):
            dve.tensor_scalar(g_qk[:, k:k + 1], vecs[:, V_QG:V_QG + 1], DA ** -0.5, None, ALU.mult)
            dve.tensor_copy(g_qk[:, 4 + k:5 + k], vecs[:, V_KG:V_KG + 1])
        dve.wait_ge(vec_T, 2)
        dve.tensor_copy(w_dw[:].rearrange("p k c -> p (k c)"), ps[:, 5, 0:KT * CONV])
        dve.wait_ge(vec_T, 3)
        dve.tensor_copy(cc_T[:].rearrange("p k c -> p (k c)"), ps[:, 6, 0:KT * PAD]).then_inc(vec_ready, 1)
        near = 384 + NREL - 1
        dve.tensor_copy(rel_u[:, 0, 0:383], rel[:, NREL - 1:NREL].to_broadcast((HA, 383))).then_inc(rel_built, 1)
        dve.tensor_copy(rel_u[:, 0, 383:near], rel[:, ::-1]).then_inc(rel_built, 1)
        dve.tensor_copy(rel_u[:, 0, near:640], rel[:, 0:1].to_broadcast((HA, 640 - near))).then_inc(rel_built, 1)
        dve.wait_ge(w_dw_hi, 1)
        dve.tensor_tensor(w_dw_l[:], w_dw[:, :, 0:PE_TAPS], w_dw_h[:].bitcast(F32), ALU.subtract)\
            .then_inc(w_dw_lo, 1)
        dve.wait_ge(wlr_hi, 1)
        dve.tensor_tensor(wlr_l[:, :, 0:RANK], wlr[:], wlr_h[:, :, 0:RANK].bitcast(F32), ALU.subtract)\
            .then_inc(wlr_lo, 1)

        def scaled(i, s, u0):
            for m in range(2):
                dve.wait_ge(gemm_done, i * 4 + (tile0(u0 + s) + m + 1))
                dve.tensor_tensor(halves(at(proj, i * 4 + (2 * (u0 + s) + m))), slot(m), halves(r_tok), ALU.mult)\
                    .then_inc(slot_free[m], 1)

        def evac_rest(i, s):
            scaled(i, s, 4)
            t = i * 2 + s
            dve.wait_ge(qk_std, t + 1)
            dve.reciprocal(rstd[:, 0:TOK], sumsq[:]).then_inc(rstd_ready, 1)
            dve.wait_ge(rstd_ready, t + 1)
            dve.scalar_tensor_tensor(out=at(proj, t), in0=at(proj, t), scalar=g_qk[:, bass.ds(t, 1)],
                                     in1=rstd[:, 0:TOK], op0=ALU.mult, op1=ALU.mult).then_inc(qk_norm, 1)

        phase(0, 4, lambda i, s: scaled(i, s, 0), first=lambda: frame_scale(0))
        phase(4, 6, evac_rest)
        split_lo(10, 0, 1)
        evac_rest(3, 0)
        evac_rest(3, 1)

        dve.wait_ge(lr_done, 1)
        dve.tensor_tensor(halves(lr[:]), ps[0:RANK, 4:6, 0:HALF], halves(r_tok)[0:RANK], ALU.mult)\
            .then_inc(lr_ready, 1)

        for g in range(1, 17, 2):
            dve.wait_ge(rows_T, g + 1)
            dst, src = rows_group(g)
            dve.tensor_copy(dst, src).then_inc(rows_out[1], 1)

        dve.wait_ge(rows_T, 15)
        for n in range(2):
            dve.wait_ge(gate_abs, n + 1)
            own(dve.tensor_scalar(halves(gl_b), sum_ps(n), vecs[:, V_GB + n:V_GB + n + 1], 0.0, ALU.add, ALU.min))
            dve.wait_ge(gate_ln, 2 * n + 1)
            dve.tensor_tensor(gl_b, gl_b, gl_a, ALU.subtract).then_inc(gate_ln, 1)
            dve.wait_ge(gate_ln, 2 * n + 2)
            for c in range(TT + 1):
                dve.tensor_tensor_scan(bt[:, n, frames(c)], ones[:, 0:width(c)], gl_b[:, frames(c)], 0.0,
                                       ALU.mult, ALU.add).then_inc(bt_ready, 1)
            dve.wait_ge(bt_ready, 5 * (n + 1))
            dve.engine_nop().then_inc(gate_min, 1)

        def biased(n):
            h, c = n // 5, n % 5
            M, nk = width(c), keys(n)
            first = 512 - nk if c < TT else 384 - PAST
            dve.wait_ge(score_done, n + 1)
            if c == 0:
                dve.wait_ge(bias_ready, h + 1)
            if n >= 4:
                dve.wait_ge(probT_done, n - 3)
            b = n % 4
            dve.tensor_tensor_reduce(prob[0:M, b, 0:nk], ps[0:M, n % 2, 0:nk], bias[0:M, h % 2, first:first + nk],
                                     1.0, -3.0e38, ALU.add, ALU.max, small[0:M, b:b + 1]).then_inc(score_read, 1)
            dve.wait_ge(score_read, n + 1)
            dve.tensor_scalar(small[0:M, 4 + b:5 + b], small[0:M, b:b + 1], -1.0, None, ALU.mult)\
                .then_inc(nmax_ready, 1)

        def normalised(n):
            M, nk, b = width(n % 5), keys(n), n % 4
            dve.wait_ge(exp_done, n + 1)
            own(dve.reciprocal(small[0:M, 12 + b:13 + b], small[0:M, 8 + b:9 + b]))
            dve.tensor_scalar(prob[0:M, b, 0:nk], prob[0:M, b, 0:nk], small[0:M, 12 + b:13 + b], None, ALU.mult)\
                .then_inc(prob_ready, 1)

        def by_halves(l):
            w = levels()[l]
            cols = slice(0, SEQ if l < 2 else TOK)
            return [t[:, :, cols].rearrange("p n (a h c) -> p n a h c", h=2, c=w) for t in (
                lev[:, l], bt, proj[:, T_KB:T_KB + 2, :], proj[:, T_QB:T_QB + 2, :])]

        def prepare_gla(n):
            if n == 4:
                dve.wait_ge(stored, 16 * 4)
            if 4 <= n < 6:
                for seg, w in ((slice(0, SEQ), P), (slice(SEQ, TOK), DEC)):
                    b = bt[:, n - 4, seg].rearrange("p (c t) -> p c t", t=w)
                    ins = dve.tensor_tensor(kd[:, n - 4, seg].rearrange("p (c t) -> p c t", t=w),
                                            b[:, :, w - 1:w].to_broadcast((P, (seg.stop - seg.start) // w, w)), b,
                                            ALU.subtract)
                ins.then_inc(kd_diff, 1)
            if 6 <= n < 20:
                l, pair = (n - 6) // 2, n % 2
                w = levels()[l]
                z, b, k, q = by_halves(l)
                ref = b[:, pair, :, 0, w - 1:w].to_broadcast((P, z.shape[2], w))
                dve.tensor_tensor(z[:, pair, :, 0, :], ref, b[:, pair, :, 0, :], ALU.subtract)
                dve.tensor_tensor(z[:, pair, :, 1, :], b[:, pair, :, 1, :], ref, ALU.subtract).then_inc(lev_diff, 1)
            if 20 <= n < 22:
                dve.wait_ge(kd_exp, n - 19)
                dve.tensor_tensor(kd[:, n - 20, :], kd[:, n - 20, :], proj[:, T_KB + n - 20, :], ALU.mult)
                dve.wait_ge(eb_ready, n - 19)
                dve.scalar_tensor_tensor(out=qe[:, n - 20, :], in0=proj[:, T_QB + n - 20, :], scalar=DKB ** -0.5,
                                         in1=eb[:, n - 20, :], op0=ALU.mult, op1=ALU.mult).then_inc(kd_ready, 1)
            if 22 <= n < 36:
                l, pair = (n - 22) // 2, n % 2
                dve.wait_ge(lev_exp, l + 1)
                z, b, k, q = by_halves(l)
                dve.tensor_tensor(z[:, pair, :, 0, :], z[:, pair, :, 0, :], k[:, pair, :, 0, :], ALU.mult)
                ins = dve.tensor_tensor(z[:, pair, :, 1, :], z[:, pair, :, 1, :], q[:, pair, :, 1, :], ALU.mult)
                if n == 35:
                    ins.then_inc(lev_ready, 1)

        for t in range(5 * HA + 2):
            if t >= 2:
                normalised(t - 2)
            if t < 5 * HA:
                biased(t)
                prepare_gla(t)

        def mask_pairs(m):
            c = m % 10 // 2
            M, l0 = width(c), (0 if c < TT else 2)
            dve.wait_ge(pairs_done, m + 1)
            src = ps[0:M, 2 * (m % 2):2 * (m % 2) + 2, :].rearrange("p a (l i) -> p (a l) i", i=P)[:, l0:8, 0:M]
            own(dve.tensor_tensor(masked[0:M, m % 2, l0:8, 0:M], src, masks[0:M, l0:8, 0:M], ALU.mult))
            if m >= 2:
                dve.wait_ge(ob_done, m - 1)
            dve.engine_nop().then_inc(masked_done, 1)
            dve.tensor_reduce(pair[0:M, m % 2, 0:M], masked[0:M, m % 2, l0:8, 0:M].rearrange("p l i -> p i l"), AX.X,
                              ALU.add).then_inc(pair_ready, 1)

        def new_state(m):
            h, c, b = 2 * (m // 10) + m % 2, m % 10 // 2, m % 2 * DKB
            dve.wait_ge(kv_done, m + 1)
            dve.wait_ge(ob_done, m + 1)
            kv = ps[b:b + DKB, 6 + m % 2, 0:DVB]
            st = (state if c < TT else state_s)[b:b + DKB, h // 2, :]
            if c == 0:
                dve.tensor_copy(st, kv).then_inc(state_ready, 1)
            else:
                last = frames(c).stop - 1
                dve.scalar_tensor_tensor(out=st, in0=st, scalar=eb[b:b + DKB, h // 2, last:last + 1], in1=kv,
                                         op0=ALU.mult, op1=ALU.add).then_inc(state_ready, 1)

        for m in range(20):
            mask_pairs(m)
            if m >= 1:
                new_state(m - 1)
        new_state(19)
        split_lo(U_OUT, 0, 0)
        dve.wait_ge(silu_done, 1)
        for h in range(HB):
            dve.wait_ge(ob_std, h + 1)
            own(dve.reciprocal(rstd[:, 0:TOK], sumsq[:]))
            o = proj[:, T_VB + h, :]
            own(dve.scalar_tensor_tensor(out=o, in0=o, scalar=vecs[:, V_ON:V_ON + 1], in1=rstd[:, 0:TOK],
                                         op0=ALU.mult, op1=ALU.mult))
            dve.tensor_tensor(o, o, proj[:, T_GB + h, :], ALU.mult).then_inc(ob_cat, 1)
        for k in range(KT):
            lo(k, X_CAT, proj[:, T_Q + k if k < 4 else T_VB + k - 4, :])

        def add_resid(u0, bias_at=None, x0=None, gain=None):
            def evacuate(i, s):
                for m in range(2):
                    k = i * 4 + (2 * s + m)
                    dve.wait_ge(gemm_done, i * 4 + (tile0(u0 + s) + m + 1))
                    r = halves(at(resid, k))
                    if bias_at is None:
                        dve.tensor_tensor(r, slot(m), r, ALU.add).then_inc(slot_free[m], 1)
                    else:
                        dve.scalar_tensor_tensor(out=r, in0=slot(m), scalar=vecs[:, bass.ds(k + bias_at, 1)], in1=r,
                                                 op0=ALU.add, op1=ALU.add).then_inc(slot_free[m], 1)
                if gain is not None:
                    for m in range(2):
                        lo_gain(i * 4 + (2 * s + m), x0, xf_l, xf_h, gain)
            return evacuate

        def hidden(layer, c, u0):
            base = 32 * layer + 8 * c

            def evacuate(i, s):
                for m in range(2):
                    t = i * 4 + (2 * s + m)
                    dve.wait_ge(gemm_done, i * 4 + (tile0(u0 + s) + m + 1))
                    dve.wait_ge(hidl_done, t + base + 1)
                    dve.scalar_tensor_tensor(out=halves(relu[:, m, :]), in0=slot(m), scalar=0.0, in1=halves(r_tok),
                                             op0=ALU.max, op1=ALU.mult).then_inc(slot_free[m], 1)
                    dve.wait_ge(hidh_done, t + (base + 1))
                    dve.tensor_tensor(at(hid_l[c % 2], t), relu2[:, m, :], at(hid_h[c % 2], t).bitcast(F32),
                                      ALU.subtract).then_inc(hidl_done, 1)
            return evacuate

        def ffn(layer, u0, last):
            for n, (way, c) in enumerate(FFN_ORDER):
                u = u0 + 4 * n
                if way == "up":
                    phase(u, 4, hidden(layer, c, u), first=(lambda: frame_scale(2 * layer + 1)) if c == 0 else None)
                elif c < NF - 1:
                    phase(u, 4, add_resid(u))
                else:
                    last(u)

        phase(U_OUT, 4, add_resid(U_OUT, None, X_FFN0, V_FFN))
        ffn(0, U_FFN0, lambda u: phase(u, 4, add_resid(u)))
        norm(2, X_MIX1, V_MIX + 8)

        dve.wait_ge(glu_edges, 3)

        def glu_conv(i, s):
            m = i * 2 + s
            dve.wait_ge(slot_free[0], m + (tile0(U_PW1) // 2 + 1))
            dve.wait_ge(gemm_done, i * 4 + (tile0(U_PW1 + s) + 2))
            u = at(glu, m)
            for to, ps_part, frames_ in ((PAD, ps[:, 2, 0:HALF], slice(0, HALF)),
                                         (PAD + HALF, ps[:, 3, 0:SEQ - HALF], slice(HALF, SEQ)),
                                         (2 * PAD + SEQ, ps[:, 3, SEQ - HALF:HALF], slice(SEQ, TOK))):
                n = frames_.stop - frames_.start
                ins = dve.scalar_tensor_tensor(out=u[:, to:to + n], in0=ps_part,
                                               scalar=vecs[:, bass.ds(m + V_B1, 1)], in1=sig[:, s, frames_],
                                               op0=ALU.add, op1=ALU.mult)
            ins.then_inc(slot_free[1], 1)
            dve.wait_ge(slot_free[1], m + (tile0(U_PW1) // 2 + 1))
            y, odd = at(cv, m), rstd[:]
            w = w_dw[:].rearrange("p k c -> p (k c)")
            taps = range(PE_TAPS, CONV)
            for n, t in enumerate(taps):
                if n == 8 and not (isinstance(m, int) and m == KT - 1):
                    split_lo(U_PW1, i, s + 2)
                to = (y, odd)[n % 2]
                tap = w[:, bass.ds(m * CONV + t, 1)]
                src = u[:, t:t + CW]
                if n == 0:
                    ins = dve.tensor_scalar(y, src, tap, vecs[:, bass.ds(m + V_BDW, 1)], ALU.mult, ALU.add)
                elif n == 1:
                    dve.wait_ge(conv_ready, m + 1)
                    ins = dve.tensor_scalar(odd, src, tap, None, ALU.mult)
                    ins.then_inc(conv_step, 1)
                    dve.wait_ge(glu_hi, m + 1)
                    dve.tensor_tensor(glu_l[:, s, :], u, glu_h[:, s, :].bitcast(F32), ALU.subtract)\
                        .then_inc(glu_lo, 1)
                    continue
                else:
                    dve.wait_ge(conv_step, m * (len(taps) + 1) + (n - 1))
                    ins = dve.scalar_tensor_tensor(out=to, in0=src, scalar=tap, in1=to, op0=ALU.mult, op1=ALU.add)
                ins.then_inc(conv_step, 1)
            dve.wait_ge(taps_done, m + 3)
            dve.wait_ge(conv_step, m * (len(taps) + 1) + len(taps))
            yh = y.rearrange("p (a t) -> p a t", a=2)
            dve.tensor_tensor(yh, sum_ps(1, CW // 2), yh, ALU.add).then_inc(conv_step, 1)
            dve.wait_ge(conv_step, m * (len(taps) + 1) + (len(taps) + 1))
            dve.tensor_tensor(y, y, odd, ALU.add).then_inc(conv_ready, 1)

        split_lo(U_PW1, 0, 1)
        with dve.Fori(0, KT // 2 - 1) as i:
            for s in range(2):
                glu_conv(i, s)
        glu_conv(KT // 2 - 1, 0)
        glu_conv(KT // 2 - 1, 1)
        dve.wait_ge(gemm_done, tile0(U_PW2))
        dve.tensor_copy(ccn[:, 1, :], flat(1)[0:PAD, :]).then_inc(slot_free[1], 1)
        dve.wait_ge(cvmean, 1)
        for k in range(KT):
            y = cv[:, k, :].rearrange("p (a t) -> p a t", a=2)
            dve.scalar_tensor_tensor(out=y, in0=sum_ps(0, CW // 2), scalar=-1.0, in1=y, op0=ALU.mult, op1=ALU.add)\
                .then_inc(cv_centred, 1)
        dve.wait_ge(cv_std, 1)
        own(dve.reciprocal(rstd[:], rstd[:]))
        for k in range(KT + 1):
            if k < KT:
                dve.tensor_tensor(cv[:, k, :], cv[:, k, :], rstd[:], ALU.mult).then_inc(cv_norm, 1)
            if k >= 1:
                lo(k - 1, X_PW2, xn[:, (k - 1) % 3, :])
        dve.wait_ge(stored, 16 * 8)
        phase(U_PW2, 4, add_resid(U_PW2, V_B2, X_FFN1, V_FFN + 8))

        def y_out(u):
            for i in range(2):
                for s in range(2):
                    if u + 2 * i + s + 1 < U_END:
                        split_lo(u, i, s + 1)
                    for m in range(2):
                        k = 4 * i + 2 * s + m
                        dve.wait_ge(gemm_done, tile0(u + 2 * i + s) + m + 1)
                        if k >= 2:
                            dve.wait_ge(y_T, k - 1)
                        dve.tensor_tensor(halves(y_fin[:, k % 2, :]), slot(m), halves(resid[:, k, :]), ALU.add)\
                            .then_inc(y_ready, 1)
                        dve.wait_ge(y_ready, k + 1)
                        dve.engine_nop().then_inc(slot_free[m], 1)

        ffn(1, U_FFN1, y_out)

    ctx.close()


_INS = ["x_prompt", "x_sample", "cache_a_k", "cache_a_v", "state_b", "cache_c", "norm_mix_g", "norm_ffn_g",
        "w_in_ab", "a_q_norm_g", "a_k_norm_g", "a_rel_bias", "b_gate_w_up", "b_gate_b", "b_out_norm_g", "w_out_ab",
        "c_w_pw1", "c_b_pw1", "c_w_dw", "c_b_dw", "c_ln_g", "c_ln_b", "c_w_pw2", "c_b_pw2", "w_ffn_up",
        "w_ffn_down"]
_OUTS = [("y_prompt", (1, 512, 1024)), ("y_sample", (1, 32, 1024)),
         ("ak_prompt", (1, 1, 512, 8, 64)), ("av_prompt", (1, 1, 512, 8, 64)),
         ("ak_sample", (1, 1, 32, 8, 64)), ("av_sample", (1, 1, 32, 8, 64)),
         ("sb_prompt", (1, 1, 4, 64, 128)), ("sb_sample", (1, 1, 4, 64, 128)),
         ("cc_prompt", (1, 1, 30, 1024)), ("cc_sample", (1, 1, 30, 1024))]


def kernel(**inputs):
    import numpy as np
    from concourse import bacc
    from concourse.bass_utils import run_bass_kernel_spmd

    nc = bacc.Bacc("TRN2", target_bir_lowering=False, num_devices=1)
    arrays, args = {}, {}
    for name in _INS:
        a = np.asarray(inputs[name])
        if name == "c_w_pw1":
            a = a.reshape(1, D, 2, KT, P)[:, :, ::-1].transpose(0, 1, 3, 2, 4).reshape(1, D, 2 * D)
        a = np.ascontiguousarray(a)
        arrays[f"in_{name}"] = a
        args[name] = nc.dram_tensor(f"in_{name}", a.shape, mybir.dt.from_np(a.dtype), kind="ExternalInput").ap()
    for name, shape in _OUTS:
        args[name] = nc.dram_tensor(f"out_{name}", shape, F32, kind="ExternalOutput").ap()
    hybrid_kernel(nc, **args)
    r = run_bass_kernel_spmd(nc, [arrays], core_ids=[0])
    return tuple(r.results[0][f"out_{name}"] for name, _ in _OUTS)
```
